# Optimizing a Trainium2 kernel written in Bass

```python
import math
import jax, jax.numpy as jnp
from jax import lax
import numpy as np

D_MODEL = 2048
BATCH = 1
SEQ = 1024
DEPTH = 1

CHUNK = 64
Q_BLOCK = 128
N_MIXERS = 4
BRANCH = D_MODEL
EPS = 1e-6
NEG_INF = -1e30
DIFF_V_DIM = 256
DIFF_HEADS = BRANCH // DIFF_V_DIM
DIFF_QK_DIM = DIFF_V_DIM // 2
BAND_HEAD_DIM = 64
BAND_HEADS = BRANCH // BAND_HEAD_DIM
BAND_PAST_CHUNKS = 8
BAND_PAST = BAND_PAST_CHUNKS * CHUNK
BAND_LEN = BAND_PAST + CHUNK
REL_CLIP = 256
FOX_HEAD_DIM = 128
FOX_HEADS = BRANCH // FOX_HEAD_DIM
POOL_WINDOWS = (2, 4, 8, 16)
POOL_GROUP = BRANCH // len(POOL_WINDOWS)

kernel_name = "hybrid_interleaved_streaming_encoder"

def rms_norm(x, g):
    xf = x.astype(jnp.float32)
    y = xf * lax.rsqrt(jnp.mean(xf * xf, axis=-1, keepdims=True) + EPS)
    return (y * g.astype(jnp.float32)).astype(x.dtype)

def proj_slice(h, w_in, i):
    return h @ w_in[:, i * BRANCH:(i + 1) * BRANCH]

def to_blocks(a, size):
    b, s = a.shape[0], a.shape[1]
    return jnp.moveaxis(a.reshape((b, s // size, size) + a.shape[2:]), 1, 0)

def from_blocks(o):
    o = jnp.moveaxis(o, 0, 1)
    return o.reshape((o.shape[0], o.shape[1] * o.shape[2]) + o.shape[3:])

def diff_attention(h, w_in, w_out, lq1, lk1, lq2, lk2, subln_g, lambda_init):
    b, s, _ = h.shape
    q = proj_slice(h, w_in, 0).reshape(b, s, DIFF_HEADS, 2, DIFF_QK_DIM)
    k = proj_slice(h, w_in, 1).reshape(b, s, DIFF_HEADS, 2, DIFF_QK_DIM)
    v = proj_slice(h, w_in, 2).reshape(b, s, DIFF_HEADS, DIFF_V_DIM)
    z = proj_slice(h, w_in, 3)
    f32 = jnp.float32
    lam = (jnp.exp(jnp.sum(lq1.astype(f32) * lk1.astype(f32)))
           - jnp.exp(jnp.sum(lq2.astype(f32) * lk2.astype(f32))) + lambda_init)
    scale = DIFF_QK_DIM ** -0.5
    key_chunk = jnp.arange(s) // CHUNK

    def block(args):
        qb, start = args
        sc = jnp.einsum('bqhmd,bkhmd->bhmqk', qb, k).astype(f32) * scale
        q_chunk = (start + jnp.arange(Q_BLOCK)) // CHUNK
        mask = key_chunk[None, :] <= q_chunk[:, None]
        p = jax.nn.softmax(jnp.where(mask[None, None, None], sc, NEG_INF), axis=-1)
        attn = p[:, :, 0] - lam * p[:, :, 1]
        return jnp.einsum('bhqk,bkhd->bqhd', attn.astype(v.dtype), v)

    starts = jnp.arange(s // Q_BLOCK) * Q_BLOCK
    o = from_blocks(lax.map(block, (to_blocks(q, Q_BLOCK), starts)))
    o = rms_norm(o, subln_g) * (1.0 - lambda_init)
    o = o.reshape(b, s, BRANCH) * jax.nn.silu(z)
    return o @ w_out

def band_attention(h, w_in, w_out, rel_table):
    b, s, _ = h.shape
    q = proj_slice(h, w_in, 0).reshape(b, s, BAND_HEADS, BAND_HEAD_DIM)
    k = proj_slice(h, w_in, 1).reshape(b, s, BAND_HEADS, BAND_HEAD_DIM)
    v = proj_slice(h, w_in, 2).reshape(b, s, BAND_HEADS, BAND_HEAD_DIM)
    z = proj_slice(h, w_in, 3)
    pad = ((0, 0), (BAND_PAST, 0), (0, 0), (0, 0))
    k_pad = jnp.pad(k, pad)
    v_pad = jnp.pad(v, pad)
    qi = jnp.arange(CHUNK)
    kj = jnp.arange(BAND_LEN)
    rel = qi[:, None] + BAND_PAST - kj[None, :]
    rel_idx = jnp.clip(rel, -REL_CLIP, REL_CLIP) + REL_CLIP
    bias = rel_table[:, rel_idx].astype(jnp.float32)
    scale = BAND_HEAD_DIM ** -0.5

    def chunk(args):
        qc, ci = args
        start = ci * CHUNK
        kb = lax.dynamic_slice_in_dim(k_pad, start, BAND_LEN, axis=1)
        vb = lax.dynamic_slice_in_dim(v_pad, start, BAND_LEN, axis=1)
        sc = jnp.einsum('bqhd,bkhd->bhqk', qc, kb).astype(jnp.float32) * scale + bias[None]
        valid = (start - BAND_PAST + kj) >= 0
        p = jax.nn.softmax(jnp.where(valid[None, None, None, :], sc, NEG_INF), axis=-1)
        return jnp.einsum('bhqk,bkhd->bqhd', p.astype(vb.dtype), vb)

    n_chunks = s // CHUNK
    o = from_blocks(lax.map(chunk, (to_blocks(q, CHUNK), jnp.arange(n_chunks))))
    o = o.reshape(b, s, BRANCH) * jax.nn.silu(z)
    return o @ w_out

def forgetting_attention(h, w_in, w_out, f_bias):
    b, s, _ = h.shape
    q = proj_slice(h, w_in, 0).reshape(b, s, FOX_HEADS, FOX_HEAD_DIM)
    k = proj_slice(h, w_in, 1).reshape(b, s, FOX_HEADS, FOX_HEAD_DIM)
    v = proj_slice(h, w_in, 2).reshape(b, s, FOX_HEADS, FOX_HEAD_DIM)
    z = proj_slice(h, w_in, 3)
    f_logit = h @ w_in[:, 4 * BRANCH:]
    log_f = jax.nn.log_sigmoid(f_logit.astype(jnp.float32) + f_bias.astype(jnp.float32))
    F = jnp.cumsum(log_f, axis=1)
    Fk = jnp.transpose(F, (0, 2, 1))
    key_pos = jnp.arange(s)
    scale = FOX_HEAD_DIM ** -0.5

    def block(args):
        qb, Fq, start = args
        sc = jnp.einsum('bqhd,bkhd->bhqk', qb, k).astype(jnp.float32) * scale
        sc = sc + jnp.transpose(Fq, (0, 2, 1))[..., None] - Fk[:, :, None, :]
        mask = key_pos[None, :] <= (start + jnp.arange(Q_BLOCK))[:, None]
        p = jax.nn.softmax(jnp.where(mask[None, None], sc, NEG_INF), axis=-1)
        return jnp.einsum('bhqk,bkhd->bqhd', p.astype(v.dtype), v)

    starts = jnp.arange(s // Q_BLOCK) * Q_BLOCK
    o = from_blocks(lax.map(block, (to_blocks(q, Q_BLOCK), to_blocks(F, Q_BLOCK), starts)))
    o = o.reshape(b, s, BRANCH) * jax.nn.silu(z)
    return o @ w_out

def multiscale_pool(h, w_in, w_out, pool_w, pool_scale):
    b, s, _ = h.shape
    u = proj_slice(h, w_in, 0)
    z = proj_slice(h, w_in, 1)
    uf = u.astype(jnp.float32)
    csum = jnp.cumsum(uf, axis=1)
    t1 = jnp.arange(s) + 1
    outs = []
    for g, win in enumerate(POOL_WINDOWS):
        sl = slice(g * POOL_GROUP, (g + 1) * POOL_GROUP)
        cg = csum[..., sl]
        shifted = jnp.pad(cg, ((0, 0), (win, 0), (0, 0)))[:, :s]
        mean = (cg - shifted) / jnp.minimum(t1, win).astype(jnp.float32)[None, :, None]
        outs.append(jnp.einsum('bsc,cd->bsd', (mean - uf[..., sl]).astype(u.dtype), pool_w[g]))
    y = jnp.concatenate(outs, axis=-1) * pool_scale
    return (y * jax.nn.silu(z)) @ w_out

def setup_inputs(seed: int = 0) -> dict:
    key = jax.random.key(seed)
    ks = jax.random.split(key, 24)
    f32 = jnp.float32

    def nrm(k, shape, scale):
        return jax.random.normal(k, shape, f32) * scale

    D, W = D_MODEL, BRANCH
    return {
        "x": nrm(ks[0], (BATCH, SEQ, D), 1.0),
        "c": nrm(ks[1], (BATCH, D), 1.0),
        "ada_w": nrm(ks[2], (DEPTH, D, 3 * D), 0.5 * D ** -0.5),
        "ada_b": nrm(ks[3], (DEPTH, 3 * D), 0.02),
        "norm_pre": 1.0 + nrm(ks[4], (DEPTH, D), 0.05),
        "norm_post": 1.0 + nrm(ks[5], (DEPTH, D), 0.05),
        "diff_w_in": nrm(ks[6], (D, 4 * W), D ** -0.5),
        "diff_w_out": nrm(ks[7], (W, D), W ** -0.5),
        "diff_lambda_q1": nrm(ks[8], (DIFF_QK_DIM,), 0.1),
        "diff_lambda_k1": nrm(ks[9], (DIFF_QK_DIM,), 0.1),
        "diff_lambda_q2": nrm(ks[10], (DIFF_QK_DIM,), 0.1),
        "diff_lambda_k2": nrm(ks[11], (DIFF_QK_DIM,), 0.1),
        "diff_subln": 1.0 + nrm(ks[12], (DIFF_V_DIM,), 0.05),
        "band_w_in": nrm(ks[13], (D, 4 * W), D ** -0.5),
        "band_w_out": nrm(ks[14], (W, D), W ** -0.5),
        "band_rel_bias": nrm(ks[15], (BAND_HEADS, 2 * REL_CLIP + 1), 0.5),
        "fox_w_in": nrm(ks[16], (D, 4 * W + FOX_HEADS), D ** -0.5),
        "fox_w_out": nrm(ks[17], (W, D), W ** -0.5),
        "fox_forget_bias": 2.0 + nrm(ks[18], (FOX_HEADS,), 0.5),
        "pool_w_in": nrm(ks[19], (D, 2 * W), D ** -0.5),
        "pool_w_out": nrm(ks[20], (W, D), W ** -0.5),
        "pool_group_w": nrm(ks[21], (len(POOL_WINDOWS), POOL_GROUP, POOL_GROUP), POOL_GROUP ** -0.5),
        "pool_scale": 1.0 + nrm(ks[22], (W,), 0.1),
    }

def reference(x, c, ada_w, ada_b, norm_pre, norm_post,
              diff_w_in, diff_w_out, diff_lambda_q1, diff_lambda_k1, diff_lambda_q2,
              diff_lambda_k2, diff_subln,
              band_w_in, band_w_out, band_rel_bias,
              fox_w_in, fox_w_out, fox_forget_bias,
              pool_w_in, pool_w_out, pool_group_w, pool_scale):
    c_act = jax.nn.silu(c)
    for i in range(DEPTH):
        mod = c_act @ ada_w[i] + ada_b[i]
        shift, scale, gate = jnp.split(mod, 3, axis=-1)
        h = rms_norm(x, norm_pre[i]) * (1.0 + scale[:, None, :]) + shift[:, None, :]
        kind = i % N_MIXERS
        if kind == 0:
            lambda_init = 0.8 - 0.6 * math.exp(-0.3 * i)
            y = diff_attention(h, diff_w_in, diff_w_out, diff_lambda_q1, diff_lambda_k1,
                               diff_lambda_q2, diff_lambda_k2, diff_subln, lambda_init)
        elif kind == 1:
            y = band_attention(h, band_w_in, band_w_out, band_rel_bias)
        elif kind == 2:
            y = forgetting_attention(h, fox_w_in, fox_w_out, fox_forget_bias)
        else:
            y = multiscale_pool(h, pool_w_in, pool_w_out, pool_group_w, pool_scale)
        x = x + gate[:, None, :] * rms_norm(y, norm_post[i])
    return x


_drawn_inputs = setup_inputs


def setup_inputs(seed=0):
    import zlib

    import numpy as np

    out = dict(_drawn_inputs(seed))
    spreads = {}
    factors = {'norm_pre': 3.249,
     'norm_post': 3.669,
     'diff_lambda_q1': 6.293,
     'diff_lambda_k1': 8.0,
     'diff_lambda_q2': 6.444,
     'diff_lambda_k2': 5.28,
     'diff_subln': 4.149}
    for name, (base, spread) in spreads.items():
        noise = np.random.default_rng([zlib.crc32(name.encode()), seed]).standard_normal(out[name].shape)
        drawn = base * np.exp(spread * noise) if base else spread * noise
        out[name] = __import__('jax').numpy.asarray(drawn.astype(out[name].dtype))
    for name, factor in factors.items():
        out[name] = (out[name] * factor).astype(out[name].dtype)
    return out
```

```python
from contextlib import ExitStack

import concourse.bass as bass
from concourse import mybir

F32 = mybir.dt.float32
F32R = mybir.dt.float32r
ALU = mybir.AluOpType
ACT = mybir.ActivationFunctionType
AX = mybir.AxisListType

P = 128
EPS = 1e-6
LAMBDA_INIT = 0.8 - 0.6
MASKED = -1e30
CHUNK = 64


def build(nc, x, c, ada_w, ada_b, norm_pre, norm_post, w_in, w_out, lq1, lk1, lq2, lk2, subln, out):
    _, SEQ, D = x.shape
    VD = subln.shape[0]
    HEADS = D // VD
    KT = D // P
    TT = SEQ // P
    HALF = SEQ // 2
    HT = HALF // P
    UK = 4
    UNITS = KT // UK
    COLS = 8
    FIRST = 3
    QKSCALE = float(lq1.shape[0]) ** -0.5
    TG = D // P
    AC = 512
    SUBS = 4
    SR = TG // SUBS
    MCH = 2 * D // AC
    GCH = D // AC
    NB = SEQ // P

    ctx = ExitStack()
    with ctx:
        def sem(name):
            return ctx.enter_context(nc.semaphore(name))

        base = [nc.sbuf_base]

        def at(name, shape, dt, where=None):
            size = 4
            for n in shape[1:]:
                size *= n
            off = base[0] if where is None else where[0]
            off = (off + 31) // 32 * 32
            t = nc.alloc_sbuf_tensor_at(name, shape, dt, offset=off)
            (base if where is None else where)[0] = off + size
            return t

        hT_hi_at = [base[0]]
        hT_hi = at("hT_hi", [P, KT, SEQ], F32R)
        hT_lo = at("hT_lo", [P, KT, SEQ], F32R)
        x_tok = at("x_tok", [P, KT, TT, P], F32, hT_hi_at)

        ident = at("ident", [P, P], F32)
        mhalf = at("mhalf", [P, TT], F32)
        w_raw = at("w_raw", [P, 4, UK, P], F32)
        w_hi = at("w_hi", [P, 2, UK, P], F32R)
        w_lo = at("w_lo", [P, 2, UK, P], F32R)
        e_at = [base[0]]
        ones = at("ones", [P, P], F32)
        rows = at("rows", [P, P], F32)
        cols = at("cols", [P, P], F32)
        inv_vd = at("inv_vd", [P, 1], F32)
        eps_c = at("eps_c", [P, 1], F32)
        craw = at("craw", [P, TG], F32)
        cexp = at("cexp", [P, TG], F32)
        cact = at("cact", [P, TG], F32)
        mod = at("mod", [P, 3 * KT], F32)
        gpT = at("gpT", [P, P], F32)
        sub8 = at("sub8", [P, 2], F32)
        lamp = at("lamp", [P, 2], F32)
        lam = at("lam", [P, 4], F32)
        mcol = at("mcol", [P, P], F32R)
        mrow = at("mrow", [P, P], F32R)
        ssx = at("ssx", [P, TT], F32)
        rsx = at("rsx", [P, TT], F32)
        ev = at("ev", [P, 2, 2, HALF], F32R)
        evf = at("evf", [P, 2, HALF], F32)
        region = base[0]

        s_at = [region]
        ada = at("ada", [P, 4, SR, AC], F32, s_at)
        acc = at("acc", [P, 2, AC], F32, s_at)
        w0_raw = at("w0_raw", [P, 2, 2, FIRST * P], F32, s_at)
        w0_hi = at("w0_hi", [P, 2, 2, FIRST * P], F32R, s_at)
        w0_lo = at("w0_lo", [P, 2, 2, FIRST * P], F32R, s_at)
        h32 = at("h32", [P, 2, SEQ], F32, s_at)

        a_at = [region]
        k_sb = at("k_sb", [P, 4, SEQ], F32R, a_at)
        v_sb = at("v_sb", [P, TT, 2, VD], F32R, a_at)
        q_sb = at("q_sb", [P, 4, P], F32R, a_at)
        z_sb = at("z_sb", [P, 2, P], F32, a_at)
        prob = at("prob", [P, 2, SEQ], F32, a_at)
        aT_hi = at("aT_hi", [P, NB, P], F32R, a_at)
        aT_lo = at("aT_lo", [P, NB, P], F32R, a_at)
        o_sb = at("o_sb", [P, VD], F32, a_at)
        osq = at("osq", [P, VD], F32, a_at)
        ozf = at("ozf", [P, 2, P], F32, a_at)
        oz = at("oz", [P, 2, 2, P], F32R, a_at)
        nmax = at("nmax", [P, 2], F32, a_at)
        lsum = at("lsum", [P, 2], F32, a_at)
        rinv = at("rinv", [P, 2], F32, a_at)
        coef = at("coef", [P, 1], F32, a_at)
        oss = at("oss", [P, 1], F32, a_at)
        oms = at("oms", [P, 1], F32, a_at)
        orr = at("orr", [P, 1], F32, a_at)
        ofac = at("ofac", [P, 1], F32, a_at)

        y_sb = at("y_sb", [P, HT, D], F32, e_at)
        x_sb = at("x_sb", [P, HT, D], F32, e_at)
        yT = at("yT", [P, 2, HALF], F32, e_at)
        gpb = at("gpb", [P, D], F32, e_at)
        ysq = at("ysq", [P, P], F32, e_at)
        yss = at("yss", [P, HT, KT], F32, e_at)
        yms = at("yms", [P, HT], F32, e_at)
        yrs = at("yrs", [P, HT], F32, e_at)
        for used in (s_at, a_at, e_at):
            assert used[0] <= nc.sbuf_usable_end, (used[0], nc.sbuf_usable_end)

        ps = ctx.enter_context(nc.psum_tensor("ps", [P, 8, HALF], F32))
        SC, VX, OB = 4, 6, 7

        def dram(name, shape):
            return nc.dram_tensor(name, shape, F32, kind="Internal").ap()

        q_dr = dram("q_dr", [HEADS * 4, P, SEQ])
        k_dr = dram("k_dr", [HEADS * 4, P, SEQ])
        v_dr = dram("v_dr", [HEADS * SEQ, 2, VD])
        z_dr = dram("z_dr", [HEADS * 2, P, SEQ])
        oz_dr = dram("oz_dr", [2, KT, P, SEQ])
        gp_dr = dram("gp_dr", [KT, P])

        rows_in, c_in = sem("rows_in"), sem("c_in")
        x_in = [sem(f"x_in{i}") for i in range(TT)]
        ada_in = [sem(f"ada_in{i}") for i in range(4)]
        w0_in = [sem(f"w0_in{i}") for i in range(2)]
        w_in_s = [sem(f"w_in{i}") for i in range(4)]
        consts = sem("consts")
        cols_t, cols_ok = sem("cols_t"), sem("cols_ok")
        lam_p, lam_mm, lam_e, lam_ok = sem("lam_p"), sem("lam_mm"), sem("lam_e"), sem("lam_ok")
        c_e, c_ok = sem("c_e"), sem("c_ok")
        x_sq, x_ms, x_rs, x_sc = sem("x_sq"), sem("x_ms"), sem("x_rs"), sem("x_sc")
        acc_ok, acc_used, mod_mm, mod_ok = sem("acc_ok"), sem("acc_used"), sem("mod_mm"), sem("mod_ok")
        mod_sum_ok = sem("mod_sum_ok")
        xT_mm, h_ok, h_hi, h_lo = sem("xT_mm"), sem("h_ok"), sem("h_hi"), sem("h_lo")
        w0_h, w0_l, w0_used = sem("w0_h"), sem("w0_l"), sem("w0_used")
        gp_ok, gp_mm, gp_cp, gp_st = sem("gp_ok"), sem("gp_mm"), sem("gp_cp"), sem("gp_st")
        w_hi_ok, w_split, w_used = sem("w_hi_ok"), sem("w_split"), sem("w_used")
        proj_done, ev_hi_ok, ev_done = sem("proj_done"), sem("ev_hi_ok"), sem("ev_done")
        z_add, z_rec = sem("z_add"), sem("z_rec")
        vt_mm, vt_hi, vt_done = sem("vt_mm"), sem("vt_hi"), sem("vt_done")
        stored = [sem("stored0"), sem("stored1")]
        q_ld, k_ld, v_ld, z_ld = sem("q_ld"), sem("k_ld"), sem("v_ld"), sem("z_ld")
        s_done, max_done, exp_done = sem("s_done"), sem("max_done"), sem("exp_done")
        rinv_ok, coef_ok, comb_done = sem("rinv_ok"), sem("coef_ok"), sem("comb_done")
        t_done, at_hi_ok, at_done = sem("t_done"), sem("at_hi_ok"), sem("at_done")
        pv_done, sq_done, fac_ok, o_ok = sem("pv_done"), sem("sq_done"), sem("fac_ok"), sem("o_ok")
        pl_mean, pl_ms, pl_rs = sem("pl_mean"), sem("pl_ms"), sem("pl_rs")
        oT_done, ozf_ok, oz_hi_ok, oz_ok, oz_st = (sem("oT_done"), sem("ozf_ok"), sem("oz_hi_ok"),
                                                   sem("oz_ok"), sem("oz_st"))
        oz_ld = [sem(f"oz_ld{i}") for i in range(UNITS)]
        gpb_in, xh_in = sem("gpb_in"), sem("xh_in")
        out_done, yT_ok, yx_done, y_ok, yss_ok = (sem("out_done"), sem("yT_ok"), sem("yx_done"),
                                                  sem("y_ok"), sem("yss_ok"))
        yms_ok, yr1, yrs_ok, fin, out_st = sem("yms_ok"), sem("yr1"), sem("yrs_ok"), sem("fin"), sem("out_st")

        ada_v = ada_w[0].rearrange("(p t) n -> p t n", t=TG)
        w_in_v = w_in.rearrange("(k p) n -> p k n", p=P)
        w_out_v = w_out.rearrange("(k p) n -> p k n", p=P)
        x_v = x[0].rearrange("(t p) (k c) -> p t k c", p=P, c=P)
        R_B, R_PRE, R_POST, R_SUB, R_LAM = 0, 3 * KT, 4 * KT, 5 * KT, 5 * KT + 2

        def unit_no(G, j):
            return (G - FIRST) * UNITS + j

        def bank_of(h, cc, half):
            if isinstance(h, int) and h == 0 and cc < FIRST:
                return cc * 2 + half
            return cc % 2 * 2 + half

        block = ctx.enter_context(nc.Block())

        @block.sync
        def _(sp):
            sp.dma_start(craw[:, :], c[0].rearrange("(p t) -> p t", t=TG)).then_inc(c_in, 16)
            sp.dma_start(rows[R_B:R_PRE, :], ada_b[0].rearrange("(r p) -> r p", p=P)).then_inc(rows_in, 16)
            sp.dma_start(rows[R_PRE:R_POST, :], norm_pre[0].rearrange("(r p) -> r p", p=P)).then_inc(rows_in, 16)
            sp.dma_start(rows[R_POST:R_SUB, :], norm_post[0].rearrange("(r p) -> r p", p=P)).then_inc(rows_in, 16)
            sp.dma_start(rows[R_SUB:R_LAM, :], subln.rearrange("(r p) -> r p", p=P)).then_inc(rows_in, 16)
            for i, v in enumerate((lq1, lk1, lq2, lk2)):
                sp.dma_start(rows[R_LAM + i:R_LAM + i + 1, :], v.rearrange("(r p) -> r p", p=P)).then_inc(rows_in, 16)
            for t in range(TT):
                sp.dma_start(x_tok[:, :, t, :], x_v[:, t]).then_inc(x_in[t], 16)

            def load_ada(s):
                ch, r = s // SUBS, s % SUBS
                if s >= 4:
                    sp.wait_ge(acc_ok, (s - 3) * SR)
                src = ada_v[:, r * SR:(r + 1) * SR]
                if ch < MCH:
                    src = src.rearrange("p t (m n) -> p t m n", m=3)[:, :, 0:2, ch * 256:(ch + 1) * 256]
                    dst = ada[:, s % 4].rearrange("p t (m n) -> p t m n", m=2)
                    for m in range(2):
                        sp.dma_start(dst[:, :, m], src[:, :, m]).then_inc(ada_in[s % 4], 16)
                else:
                    g = 2 * D + (ch - MCH) * AC
                    sp.dma_start(ada[:, s % 4], src[:, :, g:g + AC]).then_inc(ada_in[s % 4], 16)

            def load_w0(i):
                if i >= 2:
                    sp.wait_ge(w0_l, i - 1)
                sp.dma_start(w0_raw[:, i % 2, :, 0:VD], w_in_v[:, 2 * i:2 * i + 2, 0:VD]).then_inc(w0_in[i % 2], 16)
                sp.dma_start(w0_raw[:, i % 2, :, VD:FIRST * P],
                             w_in_v[:, 2 * i:2 * i + 2, D:D + FIRST * P - VD]).then_inc(w0_in[i % 2], 16)

            def w_cols(h, cc):
                part, m = cc // 2, cc % 2
                return bass.ds(h * VD + (part * D + m * P), P)

            def load_w(h, cc, j):
                n = unit_no(h * COLS + cc, j)
                if not isinstance(n, int) or n >= 4:
                    sp.wait_ge(w_split, n - 3)
                sp.dma_start(w_raw[:, j], w_in_v[:, j * UK:(j + 1) * UK, w_cols(h, cc)]).then_inc(w_in_s[j], 16)

            def store(h, cc, half):
                G, part, m = h * COLS + cc, cc // 2, cc % 2
                tok = slice(half * HALF, (half + 1) * HALF)
                if part == 2:
                    sp.wait_ge(vt_done, h * 4 + (m * 2 + half + 1))
                    dst = v_dr[bass.ds(h * SEQ + half * HALF, HALF)].rearrange("(t p) s d -> p t s d", p=P)
                    src = ev[:, half].rearrange("p s (t d) -> p t s d", t=HT).bitcast(F32)
                    for s in range(2):
                        last = sp.dma_start(dst[:, :, s, m * P:(m + 1) * P], src[:, :, s])
                        last.then_inc(stored[half], 16)
                    return
                sp.wait_ge(ev_done, G * 2 + half + 1)
                if part == 3:
                    sp.dma_start(z_dr[bass.ds(h * 2 + m, 1), :, tok].rearrange("h p n -> p h n"),
                                 evf[:, half:half + 1]).then_inc(stored[half], 32)
                else:
                    dr = (q_dr, k_dr)[part]
                    sp.dma_start(dr[bass.ds(h * 4 + m * 2, 2), :, tok].rearrange("s p n -> p s n"),
                                 ev[:, half].bitcast(F32)).then_inc(stored[half], 32)

            def load_qk(h, qb):
                a = h * NB + qb
                if qb == 0:
                    for half in range(2):
                        sp.wait_ge(stored[half], (h * COLS + 4) * 32)
                if not isinstance(a, int) or a > 0:
                    sp.wait_ge(s_done, a * 2)
                tok = slice(qb * P, (qb + 1) * P)
                hd = bass.ds(h * 4, 4)
                sp.dma_start(q_sb[:, :, :].bitcast(F32), q_dr[hd, :, tok].rearrange("s p n -> p s n")).then_inc(q_ld, 16)
                sp.dma_start(k_sb[:, :, tok].bitcast(F32), k_dr[hd, :, tok].rearrange("s p n -> p s n")).then_inc(k_ld, 16)

            def load_v(h, qb):
                a = h * NB + qb
                if qb == 0:
                    for half in range(2):
                        sp.wait_ge(stored[half], (h * COLS + 6) * 32)
                sp.wait_ge(pv_done, a)
                sp.dma_start(v_sb[:, qb].bitcast(F32),
                             v_dr[bass.ds(h * SEQ + qb * P, P)]).then_inc(v_ld, 16)

            def load_z(h, qb):
                a = h * NB + qb
                if qb == 0:
                    for half in range(2):
                        sp.wait_ge(stored[half], (h * COLS + 8) * 32)
                sp.wait_ge(ozf_ok, a)
                sp.dma_start(z_sb[:, :, :],
                             z_dr[bass.ds(h * 2, 2), :, qb * P:(qb + 1) * P].rearrange("m p n -> p m n")).then_inc(z_ld, 16)

            def store_oz(h, qb):
                a = h * NB + qb
                sp.wait_ge(oz_ok, a + 1)
                for s in range(2):
                    sp.dma_start(oz_dr[s, bass.ds(h * 2, 2), :, qb * P:(qb + 1) * P].rearrange("m p n -> p m n"),
                                 oz[:, s].bitcast(F32)).then_inc(oz_st, 16)

            def head_steps(h, first):
                for cc in range(COLS):
                    nh, ncc = (h, cc + 1) if cc + 1 < COLS else (h + 1, 0)
                    pos = (h - 1, cc)
                    load_w(nh, ncc, 0)
                    load_v(*pos)
                    load_w(nh, ncc, 1)
                    load_w(nh, ncc, 2)
                    if not (first and cc == 0):
                        store_oz(*((h - 1, cc - 1) if cc else (h - 2, NB - 1)))
                    for half in range(2):
                        store(*((h, cc - 1) if cc else (h - 1, COLS - 1)), half)
                    load_w(nh, ncc, 3)
                    load_z(*pos)
                    load_qk(*((h - 1, cc + 1) if cc + 1 < NB else (h, 0)))

            for i in range(MCH):
                load_w0(i)
                for r in range(SUBS):
                    load_ada(i * SUBS + r)
            for j in range(UNITS):
                load_w(0, FIRST, j)
            g = 0
            for cc in range(FIRST, COLS):
                for j in range(UNITS):
                    if g < GCH * SUBS:
                        load_ada(MCH * SUBS + g)
                        g += 1
                    if cc + 1 < COLS:
                        load_w(0, cc + 1, j)
                    else:
                        load_w(1, 0, j)
                    if j == 1 and cc == FIRST:
                        for c0 in range(FIRST):
                            for half in range(2):
                                store(0, c0, half)
                    if j == 2 and cc > FIRST:
                        for half in range(2):
                            store(0, cc - 1, half)
            sp.wait_ge(gp_cp, 1)
            sp.dma_start(gp_dr[:, :], gpT[0:KT, :]).then_inc(gp_st, 16)
            load_qk(0, 0)

            head_steps(1, True)
            with sp.Fori(2, HEADS - 1) as h:
                head_steps(h, False)
            LH = HEADS - 1

            def load_wo(o, j):
                sp.wait_ge(w_split, unit_no(HEADS * COLS + o, j) - 3)
                ct = o % KT if isinstance(o, int) else None
                sp.dma_start(w_raw[:, j], w_out_v[:, j * UK:(j + 1) * UK, ct * P:(ct + 1) * P]).then_inc(w_in_s[j], 16)

            for cc in range(COLS):
                def nxt(j):
                    if cc + 1 < COLS:
                        load_w(LH, cc + 1, j)
                    else:
                        load_wo(0, j)
                nxt(0)
                load_v(LH - 1, cc)
                nxt(1)
                nxt(2)
                store_oz(*((LH - 1, cc - 1) if cc else (LH - 2, NB - 1)))
                for half in range(2):
                    store(*((LH, cc - 1) if cc else (LH - 1, COLS - 1)), half)
                nxt(3)
                load_z(LH - 1, cc)
                load_qk(*((LH - 1, cc + 1) if cc + 1 < NB else (LH, 0)))

            def load_oz(j, kts):
                for kt in kts:
                    for s, t in enumerate((hT_hi, hT_lo)):
                        sp.dma_start(t[:, kt].bitcast(F32), oz_dr[s, kt]).then_inc(oz_ld[j], 16)

            for qb in range(NB):
                load_v(LH, qb)
                store_oz(*((LH, qb - 1) if qb else (LH - 1, NB - 1)))
                if qb == 0:
                    for half in range(2):
                        store(LH, COLS - 1, half)
                load_z(LH, qb)
                if qb + 1 < NB:
                    load_qk(LH, qb + 1)
                if qb == 0:
                    sp.wait_ge(proj_done, HEADS * COLS * 2)
                    sp.wait_ge(oz_st, (LH * NB) * 32)
                    for j in range(3):
                        load_oz(j, range(j * UK, (j + 1) * UK))
                    load_oz(3, range(3 * UK, 3 * UK + 2))
            store_oz(LH, NB - 1)
            sp.wait_ge(oz_st, HEADS * NB * 32)
            load_oz(3, range(3 * UK + 2, KT))
            sp.wait_ge(gp_st, 16)
            sp.dma_start(gpb[:, :], gp_dr.rearrange("k p -> (k p)")[None, :].to_broadcast([P, D])).then_inc(gpb_in, 16)
            def load_x(half):
                for t in range(HT):
                    r = (half * HT + t) * P
                    sp.dma_start(x_sb[:, t], x[0, r:r + P, :]).then_inc(xh_in, 16)

            def store_out(half):
                for t in range(HT):
                    sp.wait_ge(fin, half * HT + t + 1)
                    r = (half * HT + t) * P
                    sp.dma_start(out[0, r:r + P, :], x_sb[:, t]).then_inc(out_st, 16)

            for o in range(2 * KT):
                for j in range(UNITS):
                    if o + 1 < 2 * KT:
                        load_wo(o + 1, j)
                if o == 0:
                    load_x(0)
                if o == KT + 1:
                    store_out(0)
                if o == KT + 4:
                    sp.wait_ge(out_st, HT * 16)
                    load_x(1)
            store_out(1)
            sp.wait_ge(out_st, 2 * HT * 16)

        @block.gpsimd
        def _(pool):
            nc.gpsimd.memset(ones[:, :], 1.0).then_inc(consts, 1)
            nc.gpsimd.memset(ident[:, :], 0.0).then_inc(consts, 1)
            pool.wait_ge(consts, 2)
            nc.gpsimd.affine_select(out=ident[:, :], in_=ident[:, :], compare_op=ALU.not_equal, fill=1.0,
                                    base=0, pattern=[[-1, P]], channel_multiplier=1).then_inc(consts, 1)
            nc.gpsimd.memset(mhalf[:, :], -0.5).then_inc(consts, 1)
            nc.gpsimd.memset(mcol[0:1, :].bitcast(F32), 0.0).then_inc(consts, 1)
            nc.gpsimd.memset(mrow[0:1, :].bitcast(F32), 0.0).then_inc(consts, 1)
            pool.wait_ge(consts, 6)
            nc.gpsimd.memset(mcol[0:1, 0:CHUNK].bitcast(F32), 1.0).then_inc(consts, 1)
            nc.gpsimd.memset(mrow[0:1, CHUNK:P].bitcast(F32), MASKED).then_inc(consts, 1)
            nc.gpsimd.memset(inv_vd[:, :], 1.0 / VD).then_inc(consts, 1)
            nc.gpsimd.memset(eps_c[:, :], EPS).then_inc(consts, 1)
            pool.wait_ge(consts, 10)
            pool.wait_ge(x_sq, TT)
            nc.gpsimd.tensor_scalar(rsx[:, :], ssx[:, :], 1.0 / D, EPS, ALU.mult, ALU.add).then_inc(x_ms, 1)
            pool.wait_ge(x_ms, 1)
            nc.gpsimd.tensor_tensor(rsx[:, :], rsx[:, :], mhalf[:, :], ALU.pow).then_inc(x_rs, 1)

            def out_factor(a):
                pool.wait_ge(sq_done, a + 1)
                nc.gpsimd.tensor_tensor(oms[:, :], oss[:, :], inv_vd[:, :], ALU.mult).then_inc(pl_mean, 1)
                pool.wait_ge(pl_mean, a + 1)
                nc.gpsimd.tensor_tensor(oms[:, :], oms[:, :], eps_c[:, :], ALU.add).then_inc(pl_ms, 1)
                pool.wait_ge(pl_ms, a + 1)
                nc.gpsimd.tensor_tensor(orr[:, :], oms[:, :], mhalf[:, 0:1], ALU.pow).then_inc(pl_rs, 1)
                pool.wait_ge(pl_rs, a + 1)
                if not isinstance(a, int) or a > 0:
                    pool.wait_ge(o_ok, a)
                nc.gpsimd.tensor_tensor(ofac[:, :], orr[:, :], rinv[:, 0:1], ALU.mult).then_inc(fac_ok, 1)

            out_factor(0)
            with pool.Fori(1, HEADS * NB) as a:
                out_factor(a)
            for half in range(2):
                pool.wait_ge(yms_ok, half + 1)
                nc.gpsimd.tensor_scalar(yrs[:, :], yms[:, :], 1.0 / D, EPS, ALU.mult, ALU.add).then_inc(yr1, 1)
                pool.wait_ge(yr1, half + 1)
                nc.gpsimd.tensor_tensor(yrs[:, :], yrs[:, :], mhalf[:, 0:HT], ALU.pow).then_inc(yrs_ok, 1)

        @block.scalar
        def _(act):
            A = nc.scalar.activation

            act.wait_ge(c_in, 16)
            A(cexp[:, :], craw[:, :], ACT.Exp, scale=-1.0).then_inc(c_e, 1)
            act.wait_ge(lam_mm, 1)
            A(lam[:, 0:2], ps[:, OB, P:P + 2], ACT.Exp).then_inc(lam_e, 1)
            for t in range(TT):
                act.wait_ge(x_in[t], 16)
                if t:
                    act.wait_ge(x_sq, t)
                A(h32[:, :, :].rearrange("p a (k c) -> p (a k) c", c=P), x_tok[:, :, t, :], ACT.Square,
                  accum_out=ssx[:, t:t + 1]).then_inc(x_sq, 1)
            act.wait_ge(x_rs, 1)
            for t in range(TT):
                A(x_tok[:, :, t, :], x_tok[:, :, t, :], ACT.Copy, scale=rsx[:, t:t + 1]).then_inc(x_sc, 1)

            def h_tile(k):
                act.wait_ge(mod_ok, k // 2 + 1)
                if k >= 2:
                    act.wait_ge(h_lo, k - 1)
                for half in range(2):
                    n = 2 * k + half
                    act.wait_ge(xT_mm, n + 1)
                    A(h32[:, k % 2, half * HALF:(half + 1) * HALF], ps[:, VX], ACT.Identity,
                      scale=mod[:, KT + k:KT + k + 1], bias=mod[:, k:k + 1]).then_inc(h_ok, 1)
                act.wait_ge(h_ok, 2 * k + 2)
                A(hT_hi[:, k], h32[:, k % 2], ACT.Copy).then_inc(h_hi, 1)

            for i in range(MCH):
                act.wait_ge(w0_in[i % 2], 32 * (i // 2 + 1))
                if i >= 2:
                    act.wait_ge(w0_used, i - 1)
                A(w0_hi[:, i % 2], w0_raw[:, i % 2], ACT.Copy).then_inc(w0_h, 1)
                for k in (2 * i, 2 * i + 1):
                    h_tile(k)

            def split_w(G, j):
                n = unit_no(G, j)
                act.wait_ge(w_in_s[j], (G - FIRST + 1) * 16)
                if j == 1:
                    if isinstance(G, int) and G > HEADS * COLS:
                        act.wait_ge(out_done, G - HEADS * COLS)
                    elif not isinstance(G, int) or G > FIRST:
                        act.wait_ge(proj_done, G * 2)
                elif j >= 2 or not isinstance(G, int) or G > FIRST:
                    act.wait_ge(w_used, (G - FIRST) * (UNITS - 1) + (j - 1 if j >= 2 else 0))
                A(w_hi[:, j % 2], w_raw[:, j], ACT.Copy).then_inc(w_hi_ok, 1)

            def evict(h, cc):
                G, part = h * COLS + cc, cc // 2
                for half in range(2):
                    act.wait_ge(proj_done, G * 2 + half + 1)
                    if not isinstance(G, int) or G > 0:
                        act.wait_ge(stored[half], G * 32)
                    bank = bank_of(h, cc, half)
                    if part == 3:
                        A(evf[:, half], ps[:, bank], ACT.Exp, scale=-1.0).then_inc(ev_hi_ok, 1)
                    elif part == 2:
                        pass
                    else:
                        A(ev[:, half, 0], ps[:, bank], ACT.Copy, scale=QKSCALE if part == 0 else 1.0).then_inc(ev_hi_ok, 1)

            def v_high(h, cc, half):
                act.wait_ge(vt_mm, h * 4 + ((cc % 2) * 2 + half + 1))
                A(ev[:, half, 0], ps[:, VX], ACT.Copy).then_inc(vt_hi, 1)

            def exps(h, qb, m):
                a = h * NB + qb
                n = (qb + 1) * P
                act.wait_ge(max_done, a * 2 + m + 1)
                A(prob[:, m, 0:n], ps[:, SC:SC + 2].rearrange("p b n -> p (b n)")[:, 0:n], ACT.Exp,
                  bias=nmax[:, m:m + 1], accum_out=lsum[:, m:m + 1]).then_inc(exp_done, 1)

            def oz_high(h, qb):
                a = h * NB + qb
                act.wait_ge(ozf_ok, a + 1)
                act.wait_ge(oz_st, a * 32)
                A(oz[:, 0], ozf[:, :, :], ACT.Copy).then_inc(oz_hi_ok, 1)

            def aT_high(h, qb):
                a = h * NB + qb
                act.wait_ge(t_done, a + 1)
                A(aT_hi[:, 0:qb + 1], ps[:, SC:SC + 2].rearrange("p b (n c) -> p (b n) c", c=P)[:, 0:qb + 1],
                  ACT.Copy).then_inc(at_hi_ok, 1)

            def square(h, qb):
                a = h * NB + qb
                act.wait_ge(pv_done, a + 1)
                if not isinstance(a, int) or a > 0:
                    act.wait_ge(pl_ms, a)
                    act.wait_ge(sq_done, a)
                A(osq[:, :], ps[:, OB, 0:VD], ACT.Square, scale=rinv[:, 0:1], accum_out=oss[:, :]).then_inc(sq_done, 1)

            def step(h, cc, prev_oz):
                G = h * COLS + cc
                ph, pc = (h, cc - 1) if cc else (h - 1, COLS - 1)
                split_w(G, 1)
                exps(h - 1, cc, 0)
                evict(ph, pc)
                split_w(G, 2)
                exps(h - 1, cc, 1)
                if pc // 2 == 2:
                    v_high(ph, pc, 0)
                if prev_oz:
                    oz_high(*((h - 1, cc - 1) if cc else (h - 2, NB - 1)))
                split_w(G, 3)
                if pc // 2 == 2:
                    v_high(ph, pc, 1)
                split_w(G + 1, 0)
                aT_high(h - 1, cc)
                square(h - 1, cc)

            split_w(FIRST, 0)
            for cc in range(FIRST, COLS):
                split_w(cc, 1)
                if cc == FIRST:
                    for c0 in range(FIRST):
                        evict(0, c0)
                else:
                    evict(0, cc - 1)
                split_w(cc, 2)
                if (cc - 1) // 2 == 2:
                    v_high(0, cc - 1, 0)
                split_w(cc, 3)
                if (cc - 1) // 2 == 2:
                    v_high(0, cc - 1, 1)
                split_w(cc + 1, 0)
            for cc in range(COLS):
                step(1, cc, cc > 0)
            with act.Fori(2, HEADS) as h:
                for cc in range(COLS):
                    step(h, cc, True)
            LH = HEADS - 1
            for qb in range(NB):
                exps(LH, qb, 0)
                if qb == 0:
                    evict(LH, COLS - 1)
                exps(LH, qb, 1)
                oz_high(*((LH, qb - 1) if qb else (LH - 1, NB - 1)))
                aT_high(LH, qb)
                square(LH, qb)
            oz_high(LH, NB - 1)

            def y_square(o):
                act.wait_ge(y_ok, o + 1)
                for t in range(HT):
                    if o + t:
                        act.wait_ge(yss_ok, o * HT + t)
                    A(ysq[:, :], ps[:, VX + o % 2, t * P:(t + 1) * P], ACT.Square,
                      accum_out=yss[:, t, o % KT:o % KT + 1]).then_inc(yss_ok, 1)

            def y_evict(o):
                act.wait_ge(out_done, o + 1)
                if o >= 2:
                    act.wait_ge(yx_done, o - 1)
                A(yT[:, o % 2], ps[:, o % 4], ACT.Copy).then_inc(yT_ok, 1)

            for o in range(2 * KT):
                for j in range(1, UNITS):
                    split_w(HEADS * COLS + o, j)
                    if j == 1 and o >= 1:
                        y_evict(o - 1)
                    if j == 3 and o >= 1:
                        y_square(o - 1)
                if o + 1 < 2 * KT:
                    split_w(HEADS * COLS + o + 1, 0)
            y_evict(2 * KT - 1)
            y_square(2 * KT - 1)

        @block.vector
        def _(dve):
            V = nc.vector
            dve.wait_ge(c_e, 1)
            V.tensor_scalar(cexp[:, :], cexp[:, :], 1.0, None, ALU.add).then_inc(c_ok, 1)
            dve.wait_ge(c_ok, 1)
            V.reciprocal(cexp[:, :], cexp[:, :]).then_inc(c_ok, 1)
            dve.wait_ge(c_ok, 2)
            V.tensor_tensor(cact[:, :], craw[:, :], cexp[:, :], ALU.mult).then_inc(c_ok, 1)
            dve.wait_ge(cols_t, 1)
            V.tensor_copy(cols[:, 0:R_LAM + 4], ps[:, OB, 0:R_LAM + 4]).then_inc(cols_ok, 1)
            dve.wait_ge(cols_ok, 1)
            V.tensor_tensor(lamp[:, 0:1], cols[:, R_LAM:R_LAM + 1], cols[:, R_LAM + 1:R_LAM + 2], ALU.mult).then_inc(lam_p, 1)
            V.tensor_tensor(lamp[:, 1:2], cols[:, R_LAM + 2:R_LAM + 3], cols[:, R_LAM + 3:R_LAM + 4], ALU.mult).then_inc(lam_p, 1)
            V.tensor_scalar(sub8[:, :], cols[:, R_SUB:R_SUB + 2], 1.0 - LAMBDA_INIT, None, ALU.mult).then_inc(cols_ok, 1)
            dve.wait_ge(lam_e, 1)
            V.tensor_tensor(lam[:, 2:3], lam[:, 1:2], lam[:, 0:1], ALU.subtract).then_inc(lam_ok, 1)
            dve.wait_ge(lam_ok, 1)
            V.tensor_scalar(lam[:, 3:4], lam[:, 2:3], -LAMBDA_INIT, None, ALU.add).then_inc(lam_ok, 1)
            dve.wait_ge(c_ok, 3)

            def ada_sum(s):
                ch, r = s // SUBS, s % SUBS
                loads = sum(2 if q // SUBS < MCH else 1 for q in range(s % 4, s + 1, 4))
                dve.wait_ge(ada_in[s % 4], 16 * loads)
                if r == 0 and ch >= 2:
                    dve.wait_ge(mod_mm, ch - 1)
                for t in range(SR):
                    g = r * SR + t
                    dst, w = acc[:, ch % 2], ada[:, s % 4, t]
                    if g == 0:
                        i = V.tensor_scalar(dst, w, cact[:, g:g + 1], None, ALU.mult)
                    else:
                        dve.wait_ge(acc_ok, ch * TG + g)
                        i = V.scalar_tensor_tensor(dst, w, cact[:, g:g + 1], dst, ALU.mult, ALU.add)
                    i.then_inc(acc_ok, 1)

            def mod_cols(i):
                dve.wait_ge(mod_mm, i + 1)
                k = 2 * i
                V.tensor_tensor(mod[:, k:k + 2], ps[:, OB, 0:2], cols[:, R_B + k:R_B + k + 2], ALU.add).then_inc(mod_sum_ok, 1)
                V.scalar_tensor_tensor(mod[:, KT + k:KT + k + 2], ps[:, OB, 2:4], 1.0,
                                       cols[:, R_B + KT + k:R_B + KT + k + 2], ALU.add, ALU.add).then_inc(mod_sum_ok, 1)
                dve.wait_ge(mod_sum_ok, 2 * i + 2)
                V.tensor_tensor(mod[:, KT + k:KT + k + 2], mod[:, KT + k:KT + k + 2],
                                cols[:, R_PRE + k:R_PRE + k + 2], ALU.mult).then_inc(mod_ok, 1)

            def h_low(k):
                dve.wait_ge(h_hi, k + 1)
                V.tensor_tensor(hT_lo[:, k], h32[:, k % 2], hT_hi[:, k].bitcast(F32), ALU.subtract).then_inc(h_lo, 1)

            def w0_low(i):
                dve.wait_ge(w0_h, i + 1)
                V.tensor_tensor(w0_lo[:, i % 2], w0_raw[:, i % 2], w0_hi[:, i % 2].bitcast(F32), ALU.subtract).then_inc(w0_l, 1)

            for i in range(MCH):
                for r in range(SUBS):
                    ada_sum(i * SUBS + r)
                    if r == 1 and i:
                        h_low(2 * i - 2)
                        h_low(2 * i - 1)
                w0_low(i)
                mod_cols(i)
            h_low(KT - 2)
            h_low(KT - 1)

            def split_w(G, j):
                n = unit_no(G, j)
                dve.wait_ge(w_hi_ok, n + 1)
                V.tensor_tensor(w_lo[:, j % 2], w_raw[:, j], w_hi[:, j % 2].bitcast(F32), ALU.subtract).then_inc(w_split, 1)

            def evict(h, cc):
                G, part = h * COLS + cc, cc // 2
                for half in range(2):
                    bank = bank_of(h, cc, half)
                    src = ps[:, bank]
                    if part == 2:
                        dve.wait_ge(proj_done, G * 2 + half + 1)
                        dve.wait_ge(stored[half], G * 32)
                        V.tensor_copy(evf[:, half], src).then_inc(ev_done, 1)
                        continue
                    n = {0: 0, 1: 4, 3: 8}[part] + (cc % 2) * 2 + half + 1
                    dve.wait_ge(ev_hi_ok, h * 12 + n)
                    if part == 3:
                        e = (cc % 2) * 2 + half + 1
                        V.tensor_scalar(evf[:, half], evf[:, half], 1.0, None, ALU.add).then_inc(z_add, 1)
                        dve.wait_ge(z_add, h * 4 + e)
                        V.reciprocal(evf[:, half], evf[:, half]).then_inc(z_rec, 1)
                        dve.wait_ge(z_rec, h * 4 + e)
                        V.tensor_tensor(evf[:, half], src, evf[:, half], ALU.mult).then_inc(ev_done, 1)
                    elif part == 0:
                        V.scalar_tensor_tensor(ev[:, half, 1], src, QKSCALE, ev[:, half, 0].bitcast(F32),
                                               ALU.mult, ALU.subtract).then_inc(ev_done, 1)
                    else:
                        V.tensor_tensor(ev[:, half, 1], src, ev[:, half, 0].bitcast(F32), ALU.subtract).then_inc(ev_done, 1)

            def v_low(h, cc, half):
                dve.wait_ge(vt_hi, h * 4 + ((cc % 2) * 2 + half + 1))
                V.tensor_tensor(ev[:, half, 1], ps[:, VX], ev[:, half, 0].bitcast(F32), ALU.subtract).then_inc(vt_done, 1)

            def maxes(h, qb, m):
                a = h * NB + qb
                n = (qb + 1) * P
                dve.wait_ge(s_done, a * 2 + m + 1)
                V.tensor_reduce(out=nmax[:, m:m + 1], in_=ps[:, SC:SC + 2].rearrange("p b n -> p (b n)")[:, 0:n],
                                axis=AX.X, op=ALU.max, negate=True).then_inc(max_done, 1)

            def out_scale(h, qb):
                a = h * NB + qb
                dve.wait_ge(fac_ok, a + 1)
                if not isinstance(a, int) or a > 0:
                    dve.wait_ge(oT_done, a)
                V.tensor_scalar(o_sb[:, :], ps[:, OB, 0:VD], ofac[:, 0:1], None, ALU.mult).then_inc(o_ok, 1)

            def gate(h, qb):
                a = h * NB + qb
                dve.wait_ge(oT_done, a + 1)
                dve.wait_ge(z_ld, (a + 1) * 16)
                dve.wait_ge(oz_hi_ok, a)
                for m in range(2):
                    i = V.scalar_tensor_tensor(ozf[:, m], ps[:, OB, VD + m * P:VD + (m + 1) * P], sub8[:, m:m + 1],
                                               z_sb[:, m], ALU.mult, ALU.mult)
                i.then_inc(ozf_ok, 1)

            def oz_low(h, qb):
                a = h * NB + qb
                dve.wait_ge(oz_hi_ok, a + 1)
                V.tensor_tensor(oz[:, 1], ozf[:, :, :], oz[:, 0].bitcast(F32), ALU.subtract).then_inc(oz_ok, 1)

            def combine(h, qb):
                a = h * NB + qb
                n = (qb + 1) * P
                dve.wait_ge(exp_done, a * 2 + 2)
                V.reciprocal(rinv[:, :], lsum[:, :]).then_inc(rinv_ok, 1)
                dve.wait_ge(rinv_ok, a + 1)
                V.scalar_tensor_tensor(coef[:, :], lsum[:, 0:1], lam[:, 3:4], rinv[:, 1:2], ALU.mult, ALU.mult).then_inc(coef_ok, 1)
                dve.wait_ge(coef_ok, a + 1)
                V.scalar_tensor_tensor(prob[:, 0, 0:n], prob[:, 1, 0:n], coef[:, 0:1], prob[:, 0, 0:n],
                                       ALU.mult, ALU.add).then_inc(comb_done, 1)

            def aT_low(h, qb):
                a = h * NB + qb
                dve.wait_ge(at_hi_ok, a + 1)
                V.tensor_tensor(aT_lo[:, 0:qb + 1], ps[:, SC:SC + 2].rearrange("p b (n c) -> p (b n) c", c=P)[:, 0:qb + 1],
                                aT_hi[:, 0:qb + 1].bitcast(F32), ALU.subtract).then_inc(at_done, 1)

            def step(h, cc, prev):
                G = h * COLS + cc
                ph, pc = (h, cc - 1) if cc else (h - 1, COLS - 1)
                last = (h - 1, cc - 1) if cc else (h - 2, NB - 1)
                split_w(G, 1)
                maxes(h - 1, cc, 0)
                if prev:
                    out_scale(*last)
                evict(ph, pc)
                split_w(G, 2)
                maxes(h - 1, cc, 1)
                if prev:
                    gate(*last)
                if pc // 2 == 2:
                    v_low(ph, pc, 0)
                combine(h - 1, cc)
                if prev:
                    oz_low(*last)
                split_w(G, 3)
                if pc // 2 == 2:
                    v_low(ph, pc, 1)
                split_w(G + 1, 0)
                aT_low(h - 1, cc)

            split_w(FIRST, 0)
            it = 0
            for cc in range(FIRST, COLS):
                for j in range(1, UNITS + 1):
                    split_w(cc + j // UNITS, j % UNITS)
                    if j == 1:
                        if cc == FIRST:
                            for c0 in range(FIRST):
                                evict(0, c0)
                        else:
                            evict(0, cc - 1)
                    if (cc - 1) // 2 == 2 and j in (2, 3):
                        v_low(0, cc - 1, j - 2)
                    if it < GCH * SUBS:
                        ada_sum(MCH * SUBS + it)
                    if it % SUBS == 0 and it:
                        i = it // SUBS - 1
                        dve.wait_ge(mod_mm, MCH + i + 1)
                        k = 4 * i
                        V.tensor_tensor(mod[:, 2 * KT + k:2 * KT + k + 4], ps[:, OB, 0:4],
                                        cols[:, R_B + 2 * KT + k:R_B + 2 * KT + k + 4], ALU.add).then_inc(mod_ok, 1)
                    it += 1
            dve.wait_ge(mod_ok, MCH + GCH)
            V.tensor_tensor(mod[:, 2 * KT:3 * KT], mod[:, 2 * KT:3 * KT], cols[:, R_POST:R_POST + KT], ALU.mult).then_inc(gp_ok, 1)
            dve.wait_ge(gp_mm, 1)
            V.tensor_copy(gpT[0:KT, :], ps[0:KT, OB, 0:P]).then_inc(gp_cp, 1)

            for cc in range(COLS):
                step(1, cc, cc > 0)
            with dve.Fori(2, HEADS) as h:
                for cc in range(COLS):
                    step(h, cc, True)
            LH = HEADS - 1
            for qb in range(NB):
                last = (LH, qb - 1) if qb else (LH - 1, NB - 1)
                maxes(LH, qb, 0)
                out_scale(*last)
                if qb == 0:
                    evict(LH, COLS - 1)
                maxes(LH, qb, 1)
                gate(*last)
                combine(LH, qb)
                oz_low(*last)
                aT_low(LH, qb)
            out_scale(LH, NB - 1)
            gate(LH, NB - 1)
            oz_low(LH, NB - 1)

            def y_scale(o):
                if o == 0:
                    dve.wait_ge(gpb_in, 16)
                ct = o % KT
                dve.wait_ge(yx_done, o + 1)
                if o == KT:
                    dve.wait_ge(fin, HT)
                V.tensor_tensor(y_sb[:, :, ct * P:(ct + 1) * P], ps[:, VX + o % 2].rearrange("p (t c) -> p t c", c=P),
                                gpb[:, ct * P:(ct + 1) * P].rearrange("p (o c) -> p o c", o=1).to_broadcast([P, HT, P]),
                                ALU.mult).then_inc(y_ok, 1)

            def y_rms(half):
                dve.wait_ge(yss_ok, (half + 1) * KT * HT)
                V.tensor_reduce(out=yms[:, :], in_=yss[:, :, :], axis=AX.X, op=ALU.add).then_inc(yms_ok, 1)

            def finish(half, t):
                if t == 0:
                    dve.wait_ge(yrs_ok, half + 1)
                    dve.wait_ge(xh_in, (half + 1) * HT * 16)
                    dve.wait_ge(y_ok, (half + 1) * KT)
                V.scalar_tensor_tensor(x_sb[:, t], y_sb[:, t], yrs[:, t:t + 1], x_sb[:, t], ALU.mult, ALU.add).then_inc(fin, 1)

            for o in range(2 * KT):
                for j in range(1, UNITS):
                    split_w(HEADS * COLS + o, j)
                    if o == KT + 1:
                        for t in {1: [1], 2: [2, 3], 3: []}[j]:
                            finish(0, t)
                    if j == 2 and o >= 1:
                        y_scale(o - 1)
                if o + 1 < 2 * KT:
                    split_w(HEADS * COLS + o + 1, 0)
                if o == KT:
                    y_rms(0)
                    finish(0, 0)
            y_scale(2 * KT - 1)
            y_rms(1)
            for t in range(HT):
                finish(1, t)

        @block.tensor
        def _(pe):
            MM, TR = nc.tensor.matmul, nc.tensor.transpose
            pe.wait_ge(consts, 8)
            pe.wait_ge(rows_in, 8 * 16)
            TR(ps[:, OB, 0:R_LAM + 4], rows[0:R_LAM + 4, :], ident[0:R_LAM + 4, 0:R_LAM + 4]).then_inc(cols_t, 1)
            pe.wait_ge(lam_p, 2)
            MM(ps[:, OB, P:P + 2], ones[:, :], lamp[:, :], start=True, stop=True).then_inc(lam_mm, 1)

            def mod_sum(ch):
                pe.wait_ge(acc_ok, (ch + 1) * TG)
                if ch:
                    pe.wait_ge(mod_ok, ch)
                else:
                    pe.wait_ge(lam_e, 1)
                for b in range(4):
                    i = MM(ps[:, OB, b:b + 1], acc[:, ch % 2, b * P:(b + 1) * P], ones[:, 0:1], start=True, stop=True)
                i.then_inc(mod_mm, 1)

            def x_tiles(k, half):
                n = 2 * k + half
                if n:
                    pe.wait_ge(h_ok, n)
                for t in range(HT):
                    i = TR(ps[:, VX, t * P:(t + 1) * P], x_tok[:, k, half * HT + t], ident[:, :])
                i.then_inc(xT_mm, 1)

            def three(dst, a_hi, a_lo, b_hi, b_lo, start, stop):
                MM(dst, a_hi, b_hi, start=start, stop=False)
                MM(dst, a_hi, b_lo, start=False, stop=False)
                return MM(dst, a_lo, b_hi, start=False, stop=stop)

            pe.wait_ge(x_sc, TT)
            for i in range(MCH):
                mod_sum(i)
                for k in (2 * i, 2 * i + 1):
                    x_tiles(k, 0)
                    x_tiles(k, 1)
                pe.wait_ge(w0_l, i + 1)
                for k in (2 * i, 2 * i + 1):
                    pe.wait_ge(h_lo, k + 1)
                    for cc in range(FIRST):
                        wc = slice(cc * P, (cc + 1) * P)
                        for half in range(2):
                            tok = slice(half * HALF, (half + 1) * HALF)
                            last = three(ps[:, bank_of(0, cc, half)], w0_hi[:, i % 2, k % 2, wc], w0_lo[:, i % 2, k % 2, wc],
                                         hT_hi[:, k, tok], hT_lo[:, k, tok], k == 0, k == KT - 1)
                            if k == KT - 1:
                                last.then_inc(proj_done, 1)
                if i < MCH - 1:
                    last.then_inc(w0_used, 1)

            def unit(h, cc, j):
                G = h * COLS + cc
                n = unit_no(G, j)
                pe.wait_ge(w_split, n + 1)
                for half in range(2):
                    tok = slice(half * HALF, (half + 1) * HALF)
                    bank = bank_of(h, cc, half)
                    for kk in range(UK):
                        k = j * UK + kk
                        last = three(ps[:, bank], w_hi[:, j % 2, kk], w_lo[:, j % 2, kk], hT_hi[:, k, tok], hT_lo[:, k, tok],
                                     k == 0, k == KT - 1)
                    if j == UNITS - 1:
                        last.then_inc(proj_done, 1)
                if j < UNITS - 1:
                    last.then_inc(w_used, 1)

            def v_turn(h, cc, half):
                G = h * COLS + cc
                n = (cc % 2) * 2 + half
                pe.wait_ge(ev_done, G * 2 + half + 1)
                if not (isinstance(h, int) and h == 0 and n == 0):
                    pe.wait_ge(vt_done, h * 4 + n)
                for t in range(HT):
                    i = TR(ps[:, VX, t * P:(t + 1) * P], evf[:, half, t * P:(t + 1) * P], ident[:, :])
                i.then_inc(vt_mm, 1)

            def scores(h, qb, m):
                a = h * NB + qb
                if m == 0:
                    pe.wait_ge(q_ld, (a + 1) * 16)
                    pe.wait_ge(k_ld, (a + 1) * 16)
                    if not isinstance(a, int) or a > 0:
                        pe.wait_ge(at_done, a)
                else:
                    pe.wait_ge(exp_done, a * 2 + 1)
                n = (qb + 1) * P
                for b in range(0, n, HALF):
                    e = min(b + HALF, n)
                    dst = ps[:, SC + b // HALF, 0:e - b]
                    own = e == n
                    last = three(dst, q_sb[:, 2 * m], q_sb[:, 2 * m + 1], k_sb[:, 2 * m, b:e], k_sb[:, 2 * m + 1, b:e], True, not own)
                    if own:
                        last = MM(ps[:, SC + b // HALF, e - b - P:e - b], mcol[0:1, :], mrow[0:1, :], start=False, stop=True)
                last.then_inc(s_done, 1)

            def turn(h, qb):
                a = h * NB + qb
                pe.wait_ge(comb_done, a + 1)
                for b in range(qb + 1):
                    last = TR(ps[:, SC + b // HT, (b % HT) * P:(b % HT + 1) * P], prob[:, 0, b * P:(b + 1) * P], ident[:, :])
                last.then_inc(t_done, 1)

            def weighted(h, qb):
                a = h * NB + qb
                pe.wait_ge(at_done, a + 1)
                pe.wait_ge(v_ld, (a + 1) * 16)
                pe.wait_ge(ozf_ok, a)
                for b in range(qb + 1):
                    last = three(ps[:, OB, 0:VD], aT_hi[:, b], aT_lo[:, b], v_sb[:, b, 0], v_sb[:, b, 1], b == 0, b == qb)
                last.then_inc(pv_done, 1)

            def o_turn(h, qb):
                a = h * NB + qb
                pe.wait_ge(o_ok, a + 1)
                for m in range(2):
                    last = TR(ps[:, OB, VD + m * P:VD + (m + 1) * P], o_sb[:, m * P:(m + 1) * P], ident[:, :])
                last.then_inc(oT_done, 1)

            def step(h, cc, prev):
                ph, pc = (h, cc - 1) if cc else (h - 1, COLS - 1)
                G = h * COLS + cc
                scores(h - 1, cc, 0)
                pe.wait_ge(ev_done, (G - 1) * 2)
                unit(h, cc, 0)
                scores(h - 1, cc, 1)
                if prev:
                    o_turn(*((h - 1, cc - 1) if cc else (h - 2, NB - 1)))
                if pc // 2 == 2:
                    v_turn(ph, pc, 0)
                unit(h, cc, 1)
                if pc // 2 == 2:
                    v_turn(ph, pc, 1)
                unit(h, cc, 2)
                turn(h - 1, cc)
                unit(h, cc, 3)
                weighted(h - 1, cc)

            g = 0
            for cc in range(FIRST, COLS):
                pe.wait_ge(ev_done, 2 * (cc - 1))
                for j in range(UNITS):
                    unit(0, cc, j)
                    if (cc - 1) // 2 == 2 and j in (0, 1):
                        v_turn(0, cc - 1, j)
                    g += 1
                    if g % SUBS == 0 and g <= GCH * SUBS:
                        mod_sum(MCH + g // SUBS - 1)
            pe.wait_ge(gp_ok, 1)
            TR(ps[0:KT, OB, 0:P], mod[:, 2 * KT:3 * KT], ident[:, :]).then_inc(gp_mm, 1)
            pe.wait_ge(gp_cp, 1)
            for cc in range(COLS):
                step(1, cc, cc > 0)
            with pe.Fori(2, HEADS) as h:
                for cc in range(COLS):
                    step(h, cc, True)
            LH = HEADS - 1
            for qb in range(NB):
                scores(LH, qb, 0)
                scores(LH, qb, 1)
                o_turn(*((LH, qb - 1) if qb else (LH - 1, NB - 1)))
                turn(LH, qb)
                weighted(LH, qb)
            o_turn(LH, NB - 1)

            def y_turn(o):
                pe.wait_ge(yT_ok, o + 1)
                if o >= 2:
                    pe.wait_ge(yss_ok, (o - 1) * HT)
                for t in range(HT):
                    i = TR(ps[:, VX + o % 2, t * P:(t + 1) * P], yT[:, o % 2, t * P:(t + 1) * P], ident[:, :])
                i.then_inc(yx_done, 1)

            pe.wait_ge(ozf_ok, HEADS * NB)
            pe.wait_ge(ev_done, HEADS * COLS * 2)
            for o in range(2 * KT):
                half = o // KT
                tok = slice(half * HALF, (half + 1) * HALF)
                if o >= 4:
                    pe.wait_ge(yT_ok, o - 3)
                for j in range(UNITS):
                    if o == 0:
                        pe.wait_ge(oz_ld[j], UK * 2 * 16)
                    pe.wait_ge(w_split, unit_no(HEADS * COLS + o, j) + 1)
                    for kk in range(UK):
                        k = j * UK + kk
                        last = three(ps[:, o % 4], w_hi[:, j % 2, kk], w_lo[:, j % 2, kk], hT_hi[:, k, tok], hT_lo[:, k, tok],
                                     k == 0, k == KT - 1)
                    if j < UNITS - 1:
                        last.then_inc(w_used, 1)
                    if j == 1 and o >= 1:
                        y_turn(o - 1)
                last.then_inc(out_done, 1)
            y_turn(2 * KT - 1)


_INS = ["x", "c", "ada_w", "ada_b", "norm_pre", "norm_post", "diff_w_in", "diff_w_out", "diff_lambda_q1",
        "diff_lambda_k1", "diff_lambda_q2", "diff_lambda_k2", "diff_subln"]


def kernel(**inputs):
    import numpy as _np
    import concourse.bacc as _bacc
    from concourse import mybir as _mybir
    from concourse.bass_utils import run_bass_kernel_spmd as _run

    nc = _bacc.Bacc("TRN2", target_bir_lowering=False, num_devices=1, dynamic_dma_scratch_size=1024)
    arrays, args = {}, []
    for name in _INS:
        a = _np.ascontiguousarray(inputs[name])
        arrays[f"in_{name}_dram"] = a
        args.append(nc.dram_tensor(f"in_{name}_dram", a.shape, _mybir.dt.from_np(a.dtype), kind="ExternalInput").ap())
    out = nc.dram_tensor("out_0_dram", inputs["x"].shape, _mybir.dt.float32, kind="ExternalOutput").ap()
    build(nc, *args, out)
    r = _run(nc, [arrays], core_ids=[0])
    return r.results[0]["out_0_dram"]
```

```python
from contextlib import ExitStack

import concourse.bass as bass
from concourse import mybir

F32 = mybir.dt.float32
F32R = mybir.dt.float32r
ALU = mybir.AluOpType
ACT = mybir.ActivationFunctionType
AX = mybir.AxisListType

P = 128
EPS = 1e-6
LAMBDA_INIT = 0.8 - 0.6
MASKED = -1e30
CHUNK = 64


def build(nc, x, c, ada_w, ada_b, norm_pre, norm_post, w_in, w_out, lq1, lk1, lq2, lk2, subln, out):
    _, SEQ, D = x.shape
    VD = subln.shape[0]
    HEADS = D // VD
    KT = D // P
    TT = SEQ // P
    HALF = SEQ // 2
    HT = HALF // P
    UK = 4
    UNITS = KT // UK
    COLS = 8
    FIRST = 3
    QKSCALE = float(lq1.shape[0]) ** -0.5
    TG = D // P
    AC = 512
    SUBS = 4
    SR = TG // SUBS
    MCH = 2 * D // AC
    GCH = D // AC
    NB = SEQ // P
    AHEAD = 4

    OT = 2 * KT
    OUT = [(o, j) for j in range(UNITS - 1) for o in range(4)] + [(o, UNITS - 1) for o in range(4)]
    OUT += [(o, j) for o in range(4, OT) for j in range(UNITS)]
    END = {o: u for u, (o, j) in enumerate(OUT) if j == UNITS - 1}
    SLOTS = [(1, 1, 1), (1, 1, 1), (1, 1, 1), (1, 1, 0), (1, 2, 2), (2, 2, 2), (2, 2, 2), (2, 2, 2)]
    assert sum(SLOTS[qb][i] for qb in range(4) for i in range(3)) < 12
    EARLY = 8
    assert END[EARLY] + 3 > sum(map(sum, SLOTS)) > END[EARLY - 1]

    ctx = ExitStack()
    with ctx:
        def sem(name):
            return ctx.enter_context(nc.semaphore(name))

        base = [nc.sbuf_base]

        def at(name, shape, dt, where=None):
            size = 4
            for n in shape[1:]:
                size *= n
            off = base[0] if where is None else where[0]
            off = (off + 31) // 32 * 32
            t = nc.alloc_sbuf_tensor_at(name, shape, dt, offset=off)
            (base if where is None else where)[0] = off + size
            return t

        hT_base = (base[0] + 31) // 32 * 32
        hT_hi_at = [hT_base]
        hT_hi = at("hT_hi", [P, KT, SEQ], F32R)
        hT_lo = at("hT_lo", [P, KT, SEQ], F32R)
        x_tok = at("x_tok", [P, KT, TT, P], F32, hT_hi_at)

        ident = at("ident", [P, P], F32)
        mhalf = at("mhalf", [P, TT], F32)
        w0_raw = at("w0_raw", [P, 2, 2, FIRST * P], F32, [base[0]])
        w_raw = at("w_raw", [P, 4, UK, P], F32)
        w_hi = at("w_hi", [P, 2, UK, P], F32R)
        w_lo = at("w_lo", [P, 2, UK, P], F32R)
        e_at = [base[0]]
        ev = at("ev", [P, 2, 2, HALF], F32R)
        evf = at("evf", [P, 2, HALF], F32)
        gpb = at("gpb", [P, D], F32, e_at)
        yT = at("yT", [P, 2, HALF], F32, e_at)
        ysq = at("ysq", [P, P], F32)
        yss = at("yss", [P, HT, KT], F32)
        yms = at("yms", [P, HT], F32)
        yrs = at("yrs", [P, HT], F32)
        assert e_at[0] <= base[0]
        e_at = [base[0]]
        ones = at("ones", [P, P], F32)
        rows = at("rows", [P, P], F32)
        cols = at("cols", [P, P], F32)
        inv_vd = at("inv_vd", [P, 1], F32)
        eps_c = at("eps_c", [P, 1], F32)
        craw = at("craw", [P, TG], F32)
        cexp = at("cexp", [P, TG], F32)
        cact = at("cact", [P, TG], F32)
        mod = at("mod", [P, 3 * KT], F32)
        gpT = at("gpT", [P, P], F32)
        sub8 = at("sub8", [P, 2], F32)
        lamp = at("lamp", [P, 2], F32)
        lam = at("lam", [P, 4], F32)
        mcol = at("mcol", [P, P], F32R)
        mrow = at("mrow", [P, P], F32R)
        ssx = at("ssx", [P, TT], F32)
        rsx = at("rsx", [P, TT], F32)
        region = base[0]

        s_at = [region]
        ada = at("ada", [P, 4, SR, AC], F32, s_at)
        acc = at("acc", [P, 2, 2, AC], F32, s_at)
        ev0_at = [s_at[0]]
        w0_hi = at("w0_hi", [P, 2, 2, FIRST * P], F32R, s_at)
        w0_lo = at("w0_lo", [P, 2, 2, FIRST * P], F32R, s_at)
        h32 = at("h32", [P, 2, SEQ], F32, s_at)
        ev0 = at("ev0", [P, FIRST - 1, 2, 2, HALF], F32R, ev0_at)
        assert ev0_at[0] <= s_at[0]

        a_at = [region]
        k_sb = at("k_sb", [P, 4, SEQ], F32R, a_at)
        v_sb = at("v_sb", [P, TT, 2, VD], F32R, a_at)
        q_sb = at("q_sb", [P, 4, P], F32R, a_at)
        z_sb = at("z_sb", [P, 2, P], F32, a_at)
        prob = at("prob", [P, 2, SEQ], F32, a_at)
        aT_hi = at("aT_hi", [P, NB, P], F32R, a_at)
        aT_lo = at("aT_lo", [P, NB, P], F32R, a_at)
        o_sb = at("o_sb", [P, VD], F32, a_at)
        osq = at("osq", [P, VD], F32, a_at)
        ozf = at("ozf", [P, 2, P], F32, a_at)
        oz = at("oz", [P, 2, 2, P], F32R, a_at)
        nmax = at("nmax", [P, 2], F32, a_at)
        lsum = at("lsum", [P, 2], F32, a_at)
        rinv = at("rinv", [P, 2], F32, a_at)
        coef = at("coef", [P, 1], F32, a_at)
        oss = at("oss", [P, 1], F32, a_at)
        oms = at("oms", [P, 1], F32, a_at)
        orr = at("orr", [P, 1], F32, a_at)
        ofac = at("ofac", [P, 1], F32, a_at)

        y_sb = at("y_sb", [P, HT, D], F32, e_at)
        x_sb = at("x_sb", [P, HT, D], F32, e_at)
        hT_lo_at = [hT_hi_at[0]]
        yx = at("yx", [P, KT, SEQ], F32, hT_lo_at)
        x_late = at("x_late", [P, KT, SEQ], F32, [hT_base])
        for used in (s_at, a_at, e_at):
            assert used[0] <= nc.sbuf_usable_end, (used[0], nc.sbuf_usable_end)

        ps = ctx.enter_context(nc.psum_tensor("ps", [P, 8, HALF], F32))
        SC, VX, OB = 4, 6, 7

        def dram(name, shape):
            return nc.dram_tensor(name, shape, F32, kind="Internal").ap()

        q_dr = dram("q_dr", [HEADS * 4, P, SEQ])
        k_dr = dram("k_dr", [HEADS * 4, P, SEQ])
        v_dr = dram("v_dr", [HEADS * SEQ, 2, VD])
        z_dr = dram("z_dr", [HEADS * 2, P, SEQ])
        oz_dr = dram("oz_dr", [2, KT, P, SEQ])
        gp_dr = dram("gp_dr", [KT, P])

        rows_in, c_in = sem("rows_in"), sem("c_in")
        x_in = [sem(f"x_in{i}") for i in range(TT)]
        ada_in = [sem(f"ada_in{i}") for i in range(4)]
        w0_in = [sem(f"w0_in{i}") for i in range(2)]
        w_in_s = [sem(f"w_in{i}") for i in range(4)]
        consts = sem("consts")
        cols_t, cols_ok = sem("cols_t"), sem("cols_ok")
        lam_p, lam_mm, lam_e, lam_ok = sem("lam_p"), sem("lam_mm"), sem("lam_e"), sem("lam_ok")
        c_e, c_ok = sem("c_e"), sem("c_ok")
        x_sq, x_ms, x_rs, x_sc = sem("x_sq"), sem("x_ms"), sem("x_rs"), sem("x_sc")
        acc_ok, acc_used, mod_mm, mod_ok = sem("acc_ok"), sem("acc_used"), sem("mod_mm"), sem("mod_ok")
        mod_sum_ok = sem("mod_sum_ok")
        xT_mm, h_ok, h_hi, h_lo = sem("xT_mm"), sem("h_ok"), sem("h_hi"), sem("h_lo")
        w0_h, w0_l, w0_used = sem("w0_h"), sem("w0_l"), sem("w0_used")
        gp_ok, gp_mm, gp_cp, gp_st = sem("gp_ok"), sem("gp_mm"), sem("gp_cp"), sem("gp_st")
        w_hi_ok, w_split, w_used = sem("w_hi_ok"), sem("w_split"), sem("w_used")
        proj_done, ev_hi_ok, ev_done = sem("proj_done"), sem("ev_hi_ok"), sem("ev_done")
        oz7_ok, y_moved = sem("oz7_ok"), sem("y_moved")
        vt_mm, vt_hi, vt_done = sem("vt_mm"), sem("vt_hi"), sem("vt_done")
        stored = [sem("stored0"), sem("stored1")]
        q_ld, k_ld, v_ld, z_ld = sem("q_ld"), sem("k_ld"), sem("v_ld"), sem("z_ld")
        s_done, max_done, exp_done = sem("s_done"), sem("max_done"), sem("exp_done")
        rinv_ok, coef_ok, comb_done = sem("rinv_ok"), sem("coef_ok"), sem("comb_done")
        t_done, at_hi_ok, at_done = sem("t_done"), sem("at_hi_ok"), sem("at_done")
        pv_done, sq_done, fac_ok, o_ok = sem("pv_done"), sem("sq_done"), sem("fac_ok"), sem("o_ok")
        pl_mean, pl_ms, pl_rs = sem("pl_mean"), sem("pl_ms"), sem("pl_rs")
        oT_done, ozf_ok, oz_hi_ok, oz_ok, oz_st = (sem("oT_done"), sem("ozf_ok"), sem("oz_hi_ok"),
                                                   sem("oz_ok"), sem("oz_st"))
        oz_ld = [sem(f"oz_ld{i}") for i in range(2 * UNITS)]
        gpb_in, xh_in = sem("gpb_in"), sem("xh_in")
        out_done, yT_ok, yx_done, y_ok, yss_ok = (sem("out_done"), sem("yT_ok"), sem("yx_done"),
                                                  sem("y_ok"), sem("yss_ok"))
        yms_ok, yr1, yrs_ok, fin, out_st = sem("yms_ok"), sem("yr1"), sem("yrs_ok"), sem("fin"), sem("out_st")

        ada_v = ada_w[0].rearrange("(p t) n -> p t n", t=TG)
        w_in_v = w_in.rearrange("(k p) n -> p k n", p=P)
        w_out_v = w_out.rearrange("(k p) n -> p k n", p=P)
        x_v = x[0].rearrange("(t p) (k c) -> p t k c", p=P, c=P)
        R_B, R_PRE, R_POST, R_SUB, R_LAM = 0, 3 * KT, 4 * KT, 5 * KT, 5 * KT + 2

        def unit_no(G, j):
            return (G - FIRST) * UNITS + j

        U0 = unit_no(HEADS * COLS, 0)
        USED0 = (HEADS * COLS - FIRST) * (UNITS - 1)

        def bank_of(h, cc, half):
            if isinstance(h, int) and h == 0 and cc < FIRST:
                return (2, 0, 4)[cc] + half
            return cc % 2 * 2 + half

        block = ctx.enter_context(nc.Block())

        @block.sync
        def _(sp):
            def load_ada(s):
                ch, r = s // SUBS, s % SUBS
                if ch:
                    sp.wait_ge(acc_ok, (ch - 1) * TG + (r + 1) * SR)
                src = ada_v[:, r * SR:(r + 1) * SR]
                if ch < MCH:
                    src = src.rearrange("p t (m n) -> p t m n", m=3)[:, :, 0:2, ch * 256:(ch + 1) * 256]
                    dst = ada[:, r].rearrange("p t (m n) -> p t m n", m=2)
                    for m in range(2):
                        sp.dma_start(dst[:, :, m], src[:, :, m]).then_inc(ada_in[r], 16)
                else:
                    g = 2 * D + (ch - MCH) * AC
                    sp.dma_start(ada[:, r], src[:, :, g:g + AC]).then_inc(ada_in[r], 16)

            def load_w0(i):
                if i >= 2:
                    sp.wait_ge(w0_l, i - 1)
                sp.dma_start(w0_raw[:, i % 2, :, 0:VD], w_in_v[:, 2 * i:2 * i + 2, 0:VD]).then_inc(w0_in[i % 2], 16)
                sp.dma_start(w0_raw[:, i % 2, :, VD:FIRST * P],
                             w_in_v[:, 2 * i:2 * i + 2, D:D + FIRST * P - VD]).then_inc(w0_in[i % 2], 16)

            def w_cols(h, cc):
                part, m = cc // 2, cc % 2
                return bass.ds(h * VD + (part * D + m * P), P)

            def load_w(h, cc, j):
                n = unit_no(h * COLS + cc, j)
                if not isinstance(n, int) or n >= 4:
                    sp.wait_ge(w_split, n - 3)
                sp.dma_start(w_raw[:, j], w_in_v[:, j * UK:(j + 1) * UK, w_cols(h, cc)]).then_inc(w_in_s[j], 16)

            def store(h, cc, half):
                G, part, m = h * COLS + cc, cc // 2, cc % 2
                tok = slice(half * HALF, (half + 1) * HALF)
                if part == 2:
                    sp.wait_ge(vt_done, h * 4 + (m * 2 + half + 1))
                    dst = v_dr[bass.ds(h * SEQ + half * HALF, HALF)].rearrange("(t p) s d -> p t s d", p=P)
                    src = ev[:, half].rearrange("p s (t d) -> p t s d", t=HT).bitcast(F32)
                    for s in range(2):
                        last = sp.dma_start(dst[:, :, s, m * P:(m + 1) * P], src[:, :, s])
                        last.then_inc(stored[half], 16)
                    return
                sp.wait_ge(ev_done, G * 2 + half + 1)
                src = ev0[:, cc - 1, half] if isinstance(h, int) and h == 0 and 0 < cc < FIRST else ev[:, half]
                if part == 3:
                    sp.dma_start(z_dr[bass.ds(h * 2 + m, 1), :, tok].rearrange("h p n -> p h n"),
                                 evf[:, half:half + 1]).then_inc(stored[half], 32)
                else:
                    dr = (q_dr, k_dr)[part]
                    sp.dma_start(dr[bass.ds(h * 4 + m * 2, 2), :, tok].rearrange("s p n -> p s n"),
                                 src.bitcast(F32)).then_inc(stored[half], 32)

            def load_qk(h, qb):
                a = h * NB + qb
                if qb == 0:
                    for half in range(2):
                        sp.wait_ge(stored[half], (h * COLS + 4) * 32)
                if not isinstance(a, int) or a > 0:
                    sp.wait_ge(s_done, a * 2)
                tok = slice(qb * P, (qb + 1) * P)
                hd = bass.ds(h * 4, 4)
                sp.dma_start(q_sb[:, :, :].bitcast(F32), q_dr[hd, :, tok].rearrange("s p n -> p s n")).then_inc(q_ld, 16)
                sp.dma_start(k_sb[:, :, tok].bitcast(F32), k_dr[hd, :, tok].rearrange("s p n -> p s n")).then_inc(k_ld, 16)

            def load_v(h, qb):
                a = h * NB + qb
                if qb == 0:
                    for half in range(2):
                        sp.wait_ge(stored[half], (h * COLS + 6) * 32)
                sp.wait_ge(pv_done, a)
                sp.dma_start(v_sb[:, qb].bitcast(F32),
                             v_dr[bass.ds(h * SEQ + qb * P, P)]).then_inc(v_ld, 16)

            def load_z(h, qb):
                a = h * NB + qb
                if qb == 0:
                    for half in range(2):
                        sp.wait_ge(stored[half], (h * COLS + 8) * 32)
                sp.wait_ge(ozf_ok, a)
                sp.dma_start(z_sb[:, :, :],
                             z_dr[bass.ds(h * 2, 2), :, qb * P:(qb + 1) * P].rearrange("m p n -> p m n")).then_inc(z_ld, 16)

            def store_oz(h, qb):
                a = h * NB + qb
                sp.wait_ge(oz_ok, a + 1)
                for s in range(2):
                    sp.dma_start(oz_dr[s, bass.ds(h * 2, 2), :, qb * P:(qb + 1) * P].rearrange("m p n -> p m n"),
                                 oz[:, s].bitcast(F32)).then_inc(oz_st, 16)

            def head_steps(h, first):
                for cc in range(COLS):
                    nh, ncc = (h, cc + 1) if cc + 1 < COLS else (h + 1, 0)
                    pos = (h - 1, cc)
                    load_w(nh, ncc, 0)
                    load_v(*pos)
                    load_w(nh, ncc, 1)
                    load_w(nh, ncc, 2)
                    if not (first and cc == 0):
                        store_oz(*((h - 1, cc - 1) if cc else (h - 2, NB - 1)))
                    for half in range(2):
                        store(*((h, cc - 1) if cc else (h - 1, COLS - 1)), half)
                    load_w(nh, ncc, 3)
                    load_z(*pos)
                    load_qk(*((h - 1, cc + 1) if cc + 1 < NB else (h, 0)))

            for r in range(SUBS):
                load_ada(r)
            for t in range(TT):
                sp.dma_start(x_tok[:, :, t, :], x_v[:, t]).then_inc(x_in[t], 16)
            load_w0(0)
            for i in range(1, MCH):
                for r in range(SUBS):
                    load_ada(i * SUBS + r)
                    if r == 1:
                        load_w0(i)
            sp.wait_ge(w0_l, MCH)
            for j in range(UNITS):
                load_w(0, FIRST, j)
            g = 0
            for cc in range(FIRST, COLS):
                for j in range(UNITS):
                    if g < GCH * SUBS:
                        load_ada(MCH * SUBS + g)
                        g += 1
                    if cc + 1 < COLS:
                        load_w(0, cc + 1, j)
                    else:
                        load_w(1, 0, j)
                    if j == 1 and cc == FIRST:
                        for c0 in range(FIRST):
                            for half in range(2):
                                store(0, c0, half)
                    if j == 2 and cc > FIRST:
                        for half in range(2):
                            store(0, cc - 1, half)
            sp.wait_ge(gp_cp, 1)
            sp.dma_start(gp_dr[:, :], gpT[0:KT, :]).then_inc(gp_st, 16)
            load_qk(0, 0)

            head_steps(1, True)
            with sp.Fori(2, HEADS - 1) as h:
                head_steps(h, False)
            LH = HEADS - 1

            def load_wo(u):
                if u < len(OUT):
                    o, j = OUT[u]
                    ct = o % KT
                    sp.wait_ge(w_split, U0 + u - 3)
                    sp.dma_start(w_raw[:, u % 4],
                                 w_out_v[:, j * UK:(j + 1) * UK, ct * P:(ct + 1) * P]).then_inc(w_in_s[u % 4], 16)

            for cc in range(COLS):
                def nxt(j):
                    if cc + 1 < COLS:
                        load_w(LH, cc + 1, j)
                    else:
                        load_wo(j)
                nxt(0)
                load_v(LH - 1, cc)
                nxt(1)
                nxt(2)
                store_oz(*((LH - 1, cc - 1) if cc else (LH - 2, NB - 1)))
                for half in range(2):
                    store(*((LH, cc - 1) if cc else (LH - 1, COLS - 1)), half)
                nxt(3)
                load_z(LH - 1, cc)
                load_qk(*((LH - 1, cc + 1) if cc + 1 < NB else (LH, 0)))

            def load_oz(half, j):
                tok = slice(half * HALF, (half + 1) * HALF)
                kts = slice(j * UK, min((j + 1) * UK, KT - 2))
                for s, t in enumerate((hT_hi, hT_lo)):
                    sp.dma_start(t[:, kts, tok].bitcast(F32),
                                 oz_dr[s, kts, :, tok].rearrange("k p n -> p k n")).then_inc(oz_ld[half * UNITS + j], 16)

            u = 4
            for qb in range(NB):
                load_v(LH, qb)
                for i in range(3):
                    for _ in range(SLOTS[qb][i]):
                        load_wo(u)
                        u += 1
                    if i == 0:
                        if qb == 0:
                            sp.wait_ge(proj_done, HEADS * COLS * 2)
                            sp.wait_ge(oz_st, ((LH - 1) * NB + HT) * 32)
                            load_oz(0, 0)
                            for half in range(2):
                                store(LH, COLS - 1, half)
                            load_oz(0, 1)
                        if qb in (1, 2):
                            load_oz(0, qb + 1)
                        if qb == 3:
                            for half in range(2):
                                sp.wait_ge(stored[half], HEADS * COLS * 32)
                            sp.wait_ge(gp_st, 16)
                            sp.dma_start(gpb[:, :], gp_dr.rearrange("k p -> (k p)")[None, :].to_broadcast([P, D])).then_inc(gpb_in, 16)
                    if i == 1:
                        if qb == 0:
                            store_oz(LH - 1, NB - 1)
                        load_z(LH, qb)
                        if qb + 1 < NB:
                            load_qk(LH, qb + 1)

            def load_x(half):
                for t in range(HT):
                    r = (half * HT + t) * P
                    if half:
                        sp.dma_start(x_late[:, :, t * P:(t + 1) * P],
                                     x[0, r:r + P, :].rearrange("p (k c) -> p k c", c=P)).then_inc(xh_in, 16)
                    else:
                        sp.dma_start(x_sb[:, t], x[0, r:r + P, :]).then_inc(xh_in, 16)

            def store_out(half):
                for t in range(HT):
                    sp.wait_ge(fin, half * HT + t + 1)
                    r = (half * HT + t) * P
                    if half:
                        sp.dma_start(out[0, r:r + P, :].rearrange("p (k c) -> p k c", c=P),
                                     x_late[:, :, t * P:(t + 1) * P]).then_inc(out_st, 16)
                    else:
                        sp.dma_start(out[0, r:r + P, :], x_sb[:, t]).then_inc(out_st, 16)

            moved = u - 4
            for u in range(moved, len(OUT) + 3):
                load_wo(u + 4)
                if u == moved + 2:
                    sp.wait_ge(y_moved, 1)
                    sp.wait_ge(oz7_ok, NB)
                    sp.wait_ge(oz_st, LH * NB * 32)
                    load_x(0)
                if moved + 3 <= u < moved + 3 + UNITS:
                    load_oz(1, u - moved - 3)
                if u == END[KT - 1] + 3:
                    sp.wait_ge(w_used, USED0 + END[KT - 1] + 1)
                    load_x(1)
                if u == END[KT - 1] + 9:
                    store_out(0)
            store_out(1)
            sp.wait_ge(out_st, 2 * HT * 16)

        @block.gpsimd
        def _(pool):
            nc.gpsimd.memset(ones[:, :], 1.0).then_inc(consts, 1)
            nc.gpsimd.memset(ident[:, :], 0.0).then_inc(consts, 1)
            pool.wait_ge(consts, 2)
            nc.gpsimd.affine_select(out=ident[:, :], in_=ident[:, :], compare_op=ALU.not_equal, fill=1.0,
                                    base=0, pattern=[[-1, P]], channel_multiplier=1).then_inc(consts, 1)
            nc.gpsimd.memset(mhalf[:, :], -0.5).then_inc(consts, 1)
            nc.gpsimd.memset(mcol[0:1, :].bitcast(F32), 0.0).then_inc(consts, 1)
            nc.gpsimd.memset(mrow[0:1, :].bitcast(F32), 0.0).then_inc(consts, 1)
            pool.wait_ge(consts, 6)
            nc.gpsimd.memset(mcol[0:1, 0:CHUNK].bitcast(F32), 1.0).then_inc(consts, 1)
            nc.gpsimd.memset(mrow[0:1, CHUNK:P].bitcast(F32), MASKED).then_inc(consts, 1)
            nc.gpsimd.memset(inv_vd[:, :], 1.0 / VD).then_inc(consts, 1)
            nc.gpsimd.memset(eps_c[:, :], EPS).then_inc(consts, 1)
            pool.wait_ge(consts, 10)
            for t in range(TT):
                col = slice(t, t + 1)
                pool.wait_ge(x_sq, t + 1)
                nc.gpsimd.tensor_scalar(rsx[:, col], ssx[:, col], 1.0 / D, EPS, ALU.mult, ALU.add).then_inc(x_ms, 1)
                pool.wait_ge(x_ms, t + 1)
                nc.gpsimd.tensor_tensor(rsx[:, col], rsx[:, col], mhalf[:, col], ALU.pow).then_inc(x_rs, 1)

            def w0_low(i):
                pool.wait_ge(w0_h, i + 1)
                nc.gpsimd.tensor_tensor(w0_lo[:, i % 2], w0_raw[:, i % 2], w0_hi[:, i % 2].bitcast(F32),
                                        ALU.subtract).then_inc(w0_l, 1)

            w0_low(0)
            for k in range(KT):
                for half in range(2):
                    tok = slice(half * HALF, (half + 1) * HALF)
                    pool.wait_ge(h_hi, 2 * k + half + 1)
                    nc.gpsimd.tensor_tensor(hT_lo[:, k, tok], h32[:, k % 2, tok], hT_hi[:, k, tok].bitcast(F32),
                                            ALU.subtract).then_inc(h_lo, 1)
                if k % 2 and k + 1 < KT:
                    w0_low((k + 1) // 2)

            def out_factor(a):
                pool.wait_ge(sq_done, a + 1)
                nc.gpsimd.tensor_tensor(oms[:, :], oss[:, :], inv_vd[:, :], ALU.mult).then_inc(pl_mean, 1)
                pool.wait_ge(pl_mean, a + 1)
                nc.gpsimd.tensor_tensor(oms[:, :], oms[:, :], eps_c[:, :], ALU.add).then_inc(pl_ms, 1)
                pool.wait_ge(pl_ms, a + 1)
                nc.gpsimd.tensor_tensor(orr[:, :], oms[:, :], mhalf[:, 0:1], ALU.pow).then_inc(pl_rs, 1)
                pool.wait_ge(pl_rs, a + 1)
                if not isinstance(a, int) or a > 0:
                    pool.wait_ge(o_ok, a)
                nc.gpsimd.tensor_tensor(ofac[:, :], orr[:, :], rinv[:, 0:1], ALU.mult).then_inc(fac_ok, 1)

            out_factor(0)
            with pool.Fori(1, HEADS * NB) as a:
                out_factor(a)
            for half in range(2):
                pool.wait_ge(yms_ok, half + 1)
                nc.gpsimd.tensor_scalar(yrs[:, :], yms[:, :], 1.0 / D, EPS, ALU.mult, ALU.add).then_inc(yr1, 1)
                pool.wait_ge(yr1, half + 1)
                nc.gpsimd.tensor_tensor(yrs[:, :], yrs[:, :], mhalf[:, 0:HT], ALU.pow).then_inc(yrs_ok, 1)

        @block.scalar
        def _(act):
            A = nc.scalar.activation

            act.dma_start(craw[:, :], c[0].rearrange("(p t) -> p t", t=TG)).then_inc(c_in, 16)
            for lo, hi, v in ((R_B, R_PRE, ada_b[0]), (R_PRE, R_POST, norm_pre[0]), (R_POST, R_SUB, norm_post[0]),
                              (R_SUB, R_LAM, subln), (R_LAM, R_LAM + 1, lq1), (R_LAM + 1, R_LAM + 2, lk1),
                              (R_LAM + 2, R_LAM + 3, lq2), (R_LAM + 3, R_LAM + 4, lk2)):
                act.dma_start(rows[lo:hi, :], v.rearrange("(r p) -> r p", p=P)).then_inc(rows_in, 16)
            act.wait_ge(c_in, 16)
            A(cexp[:, :], craw[:, :], ACT.Exp, scale=-1.0).then_inc(c_e, 1)
            for t in range(TT):
                if t == 1:
                    act.wait_ge(lam_mm, 1)
                    A(lam[:, 0:2], ps[:, OB, P:P + 2], ACT.Exp).then_inc(lam_e, 1)
                act.wait_ge(x_in[t], 16)
                if t:
                    act.wait_ge(x_sq, t)
                A(h32[:, :, :].rearrange("p a (k c) -> p (a k) c", c=P), x_tok[:, :, t, :], ACT.Square,
                  accum_out=ssx[:, t:t + 1]).then_inc(x_sq, 1)
            act.wait_ge(x_sq, TT)

            def h_tile(k):
                act.wait_ge(mod_ok, k // 2 + 1)
                for half in range(2):
                    n = 2 * k + half
                    tok = slice(half * HALF, (half + 1) * HALF)
                    if k >= 2:
                        act.wait_ge(h_lo, n - 3)
                    act.wait_ge(xT_mm, n + 1)
                    A(h32[:, k % 2, tok], ps[:, VX], ACT.Identity,
                      scale=mod[:, KT + k:KT + k + 1], bias=mod[:, k:k + 1]).then_inc(h_ok, 1)
                    act.wait_ge(h_ok, n + 1)
                    A(hT_hi[:, k, tok], h32[:, k % 2, tok], ACT.Copy).then_inc(h_hi, 1)

            def w0_high(i):
                act.wait_ge(w0_in[i % 2], 32 * (i // 2 + 1))
                if i >= 2:
                    act.wait_ge(w0_used, i - 1)
                A(w0_hi[:, i % 2], w0_raw[:, i % 2], ACT.Copy).then_inc(w0_h, 1)

            w0_high(0)
            for k in range(KT):
                h_tile(k)
                if k % 2 and k + 1 < KT:
                    w0_high((k + 1) // 2)

            def split_w(G, j):
                n = unit_no(G, j)
                act.wait_ge(w_in_s[j], (G - FIRST + 1) * 16)
                if j == 1:
                    if not isinstance(G, int) or G > FIRST:
                        act.wait_ge(proj_done, G * 2)
                elif j >= 2 or not isinstance(G, int) or G > FIRST:
                    act.wait_ge(w_used, (G - FIRST) * (UNITS - 1) + (j - 1 if j >= 2 else 0))
                A(w_hi[:, j % 2], w_raw[:, j], ACT.Copy).then_inc(w_hi_ok, 1)

            def evict(h, cc):
                G, part = h * COLS + cc, cc // 2
                for half in range(2):
                    if part == 2:
                        continue
                    early = isinstance(h, int) and h == 0 and cc < FIRST
                    if early and cc:
                        act.wait_ge(proj_done, FIRST * 2)
                    elif early:
                        act.wait_ge(proj_done, half + 1)
                    else:
                        act.wait_ge(proj_done, G * 2 + half + 1)
                        act.wait_ge(stored[half], G * 32)
                    src = ps[:, bank_of(h, cc, half)]
                    if part == 3:
                        A(evf[:, half], src, ACT.Tanh, scale=0.5).then_inc(ev_hi_ok, 1)
                    else:
                        dst = ev0[:, cc - 1, half, 0] if early and cc else ev[:, half, 0]
                        A(dst, src, ACT.Copy, scale=QKSCALE if part == 0 else 1.0).then_inc(ev_hi_ok, 1)

            def v_high(h, cc, half):
                act.wait_ge(vt_mm, h * 4 + ((cc % 2) * 2 + half + 1))
                A(ev[:, half, 0], ps[:, VX], ACT.Copy).then_inc(vt_hi, 1)

            def exps(h, qb, m):
                a = h * NB + qb
                n = (qb + 1) * P
                act.wait_ge(max_done, a * 2 + m + 1)
                A(prob[:, m, 0:n], ps[:, SC:SC + 2].rearrange("p b n -> p (b n)")[:, 0:n], ACT.Exp,
                  bias=nmax[:, m:m + 1], accum_out=lsum[:, m:m + 1]).then_inc(exp_done, 1)

            def oz_high(h, qb):
                a = h * NB + qb
                act.wait_ge(ozf_ok, a + 1)
                if isinstance(h, int) and h == HEADS - 1:
                    dst = hT_hi[:, KT - 2:KT, qb * P:(qb + 1) * P]
                else:
                    dst = oz[:, 0]
                    act.wait_ge(oz_st, a * 32)
                A(dst, ozf[:, :, :], ACT.Copy).then_inc(oz_hi_ok, 1)

            def aT_high(h, qb):
                a = h * NB + qb
                act.wait_ge(t_done, a + 1)
                A(aT_hi[:, 0:qb + 1], ps[:, SC:SC + 2].rearrange("p b (n c) -> p (b n) c", c=P)[:, 0:qb + 1],
                  ACT.Copy).then_inc(at_hi_ok, 1)

            def square(h, qb):
                a = h * NB + qb
                act.wait_ge(pv_done, a + 1)
                if not isinstance(a, int) or a > 0:
                    act.wait_ge(pl_ms, a)
                    act.wait_ge(sq_done, a)
                A(osq[:, :], ps[:, OB, 0:VD], ACT.Square, scale=rinv[:, 0:1], accum_out=oss[:, :]).then_inc(sq_done, 1)

            def step(h, cc, prev_oz):
                G = h * COLS + cc
                ph, pc = (h, cc - 1) if cc else (h - 1, COLS - 1)
                split_w(G, 1)
                exps(h - 1, cc, 0)
                evict(ph, pc)
                split_w(G, 2)
                exps(h - 1, cc, 1)
                if pc // 2 == 2:
                    v_high(ph, pc, 0)
                if prev_oz:
                    oz_high(*((h - 1, cc - 1) if cc else (h - 2, NB - 1)))
                split_w(G, 3)
                if pc // 2 == 2:
                    v_high(ph, pc, 1)
                split_w(G + 1, 0)
                aT_high(h - 1, cc)
                square(h - 1, cc)

            split_w(FIRST, 0)
            for cc in range(FIRST, COLS):
                if cc == FIRST:
                    for c0 in range(FIRST):
                        evict(0, c0)
                        if c0 == 0:
                            split_w(cc, 1)
                else:
                    split_w(cc, 1)
                    evict(0, cc - 1)
                split_w(cc, 2)
                if (cc - 1) // 2 == 2:
                    v_high(0, cc - 1, 0)
                split_w(cc, 3)
                if (cc - 1) // 2 == 2:
                    v_high(0, cc - 1, 1)
                split_w(cc + 1, 0)
            for cc in range(COLS):
                step(1, cc, cc > 0)
            with act.Fori(2, HEADS) as h:
                for cc in range(COLS):
                    step(h, cc, True)
            LH = HEADS - 1

            def y_square(o):
                act.wait_ge(y_ok, o + 1)
                if o == KT:
                    act.wait_ge(yms_ok, 1)
                for t in range(HT):
                    if o + t:
                        act.wait_ge(yss_ok, o * HT + t)
                    A(ysq[:, :], ps[:, VX, t * P:(t + 1) * P], ACT.Square,
                      accum_out=yss[:, t, o % KT:o % KT + 1]).then_inc(yss_ok, 1)

            def y_evict(o):
                act.wait_ge(w_used, USED0 + END[o] + 1)
                if o == 0:
                    for half in range(2):
                        act.wait_ge(stored[half], HEADS * COLS * 32)
                if o >= 2:
                    act.wait_ge(yx_done, o - 1)
                A(yT[:, o % 2], ps[:, o % 4], ACT.Copy).then_inc(yT_ok, 1)

            def tick(u):
                n = u + 1
                if n < len(OUT):
                    act.wait_ge(w_in_s[n % 4], (HEADS * COLS - FIRST + n // 4 + 1) * 16)
                    if n == 1:
                        act.wait_ge(proj_done, HEADS * COLS * 2)
                    else:
                        act.wait_ge(w_used, USED0 + n - 1)
                    A(w_hi[:, n % 2], w_raw[:, n % 4], ACT.Copy).then_inc(w_hi_ok, 1)
                for o in range(OT):
                    if END[o] == u - 1:
                        y_evict(o)
                    if END[o] == u - 3:
                        y_square(o)

            u = 0
            for qb in range(NB):
                n0, n1, n2 = SLOTS[qb]
                exps(LH, qb, 0)
                for i in range(n0):
                    tick(u + i)
                    if i == 0 and qb == 0:
                        evict(LH, COLS - 1)
                exps(LH, qb, 1)
                for i in range(n1):
                    tick(u + n0 + i)
                    if i == 0:
                        oz_high(*((LH, qb - 1) if qb else (LH - 1, NB - 1)))
                aT_high(LH, qb)
                for i in range(n2):
                    tick(u + n0 + n1 + i)
                square(LH, qb)
                u += n0 + n1 + n2
            tick(u)
            oz_high(LH, NB - 1)
            for v in range(u + 1, len(OUT) + 3):
                tick(v)

        @block.vector
        def _(dve):
            V = nc.vector
            def x_scale(t):
                dve.wait_ge(x_rs, t + 1)
                V.tensor_scalar(x_tok[:, :, t, :], x_tok[:, :, t, :], rsx[:, t:t + 1], None, ALU.mult).then_inc(x_sc, 1)

            dve.wait_ge(c_e, 1)
            V.tensor_scalar(cexp[:, :], cexp[:, :], 1.0, None, ALU.add).then_inc(c_ok, 1)
            dve.wait_ge(c_ok, 1)
            V.reciprocal(cexp[:, :], cexp[:, :]).then_inc(c_ok, 1)
            dve.wait_ge(c_ok, 2)
            V.tensor_tensor(cact[:, :], craw[:, :], cexp[:, :], ALU.mult).then_inc(c_ok, 1)
            dve.wait_ge(c_ok, 3)

            def ada_rows(lo, hi):
                for n in range(lo, hi):
                    ch, g = n // TG, n % TG
                    r, t = g // SR, g % SR
                    if t == 0:
                        loads = 2 * min(ch + 1, MCH) + max(ch + 1 - MCH, 0)
                        dve.wait_ge(ada_in[r], 16 * loads)
                    if g == 0 and ch >= 2:
                        dve.wait_ge(mod_mm, ch - 1)
                    dst, w = acc[:, ch % 2, g % 2], ada[:, r, t]
                    if g < 2:
                        i = V.tensor_scalar(dst, w, cact[:, g:g + 1], None, ALU.mult)
                    else:
                        dve.wait_ge(acc_ok, n - 1)
                        i = V.scalar_tensor_tensor(dst, w, cact[:, g:g + 1], dst, ALU.mult, ALU.add)
                    i.then_inc(acc_ok, 1)

            def mod_cols(i):
                dve.wait_ge(mod_mm, i + 1)
                k = 2 * i
                V.tensor_tensor(mod[:, k:k + 2], ps[:, OB, 0:2], cols[:, R_B + k:R_B + k + 2], ALU.add).then_inc(mod_sum_ok, 1)
                V.scalar_tensor_tensor(mod[:, KT + k:KT + k + 2], ps[:, OB, 2:4], 1.0,
                                       cols[:, R_B + KT + k:R_B + KT + k + 2], ALU.add, ALU.add).then_inc(mod_sum_ok, 1)
                dve.wait_ge(mod_sum_ok, 2 * i + 2)
                V.tensor_tensor(mod[:, KT + k:KT + k + 2], mod[:, KT + k:KT + k + 2],
                                cols[:, R_PRE + k:R_PRE + k + 2], ALU.mult).then_inc(mod_ok, 1)

            ada_rows(0, SR)
            dve.wait_ge(cols_t, 1)
            V.tensor_copy(cols[:, 0:R_LAM + 4], ps[:, OB, 0:R_LAM + 4]).then_inc(cols_ok, 1)
            dve.wait_ge(cols_ok, 1)
            V.tensor_tensor(lamp[:, 0:1], cols[:, R_LAM:R_LAM + 1], cols[:, R_LAM + 1:R_LAM + 2], ALU.mult).then_inc(lam_p, 1)
            V.tensor_tensor(lamp[:, 1:2], cols[:, R_LAM + 2:R_LAM + 3], cols[:, R_LAM + 3:R_LAM + 4], ALU.mult).then_inc(lam_p, 1)
            V.tensor_scalar(sub8[:, :], cols[:, R_SUB:R_SUB + 2], (1.0 - LAMBDA_INIT) / 2, None, ALU.mult).then_inc(cols_ok, 1)
            ada_rows(SR, TG)
            dve.wait_ge(lam_e, 1)
            V.tensor_tensor(lam[:, 2:3], lam[:, 1:2], lam[:, 0:1], ALU.subtract).then_inc(lam_ok, 1)
            dve.wait_ge(lam_ok, 1)
            V.tensor_scalar(lam[:, 3:4], lam[:, 2:3], -LAMBDA_INIT, None, ALU.add).then_inc(lam_ok, 1)
            for t in range(TT):
                x_scale(t)
                if t == 0:
                    mod_cols(0)
            for i in range(1, MCH):
                ada_rows(i * TG + (AHEAD if i > 1 else 0), (i + 1) * TG)
                if i + 1 < MCH:
                    ada_rows((i + 1) * TG, (i + 1) * TG + AHEAD)
                mod_cols(i)

            def split_w(G, j):
                n = unit_no(G, j)
                dve.wait_ge(w_hi_ok, n + 1)
                V.tensor_tensor(w_lo[:, j % 2], w_raw[:, j], w_hi[:, j % 2].bitcast(F32), ALU.subtract).then_inc(w_split, 1)

            def evict(h, cc):
                G, part = h * COLS + cc, cc // 2
                for half in range(2):
                    src = ps[:, bank_of(h, cc, half)]
                    buf = ev0[:, cc - 1, half] if isinstance(h, int) and h == 0 and 0 < cc < FIRST else ev[:, half]
                    if part == 2:
                        dve.wait_ge(proj_done, G * 2 + half + 1)
                        dve.wait_ge(stored[half], G * 32)
                        V.tensor_copy(evf[:, half], src).then_inc(ev_done, 1)
                        continue
                    n = {0: 0, 1: 4, 3: 8}[part] + (cc % 2) * 2 + half + 1
                    dve.wait_ge(ev_hi_ok, h * 12 + n)
                    if part == 3:
                        V.scalar_tensor_tensor(evf[:, half], evf[:, half], 1.0, src, ALU.add, ALU.mult).then_inc(ev_done, 1)
                    elif part == 0:
                        V.scalar_tensor_tensor(buf[:, 1], src, QKSCALE, buf[:, 0].bitcast(F32),
                                               ALU.mult, ALU.subtract).then_inc(ev_done, 1)
                    else:
                        V.tensor_tensor(buf[:, 1], src, buf[:, 0].bitcast(F32), ALU.subtract).then_inc(ev_done, 1)

            def v_low(h, cc, half):
                dve.wait_ge(vt_hi, h * 4 + ((cc % 2) * 2 + half + 1))
                V.tensor_tensor(ev[:, half, 1], ps[:, VX], ev[:, half, 0].bitcast(F32), ALU.subtract).then_inc(vt_done, 1)

            def maxes(h, qb, m):
                a = h * NB + qb
                n = (qb + 1) * P
                dve.wait_ge(s_done, a * 2 + m + 1)
                V.tensor_reduce(out=nmax[:, m:m + 1], in_=ps[:, SC:SC + 2].rearrange("p b n -> p (b n)")[:, 0:n],
                                axis=AX.X, op=ALU.max, negate=True).then_inc(max_done, 1)

            def out_scale(h, qb):
                a = h * NB + qb
                dve.wait_ge(fac_ok, a + 1)
                if not isinstance(a, int) or a > 0:
                    dve.wait_ge(oT_done, a)
                V.tensor_scalar(o_sb[:, :], ps[:, OB, 0:VD], ofac[:, 0:1], None, ALU.mult).then_inc(o_ok, 1)

            def gate(h, qb):
                a = h * NB + qb
                dve.wait_ge(oT_done, a + 1)
                dve.wait_ge(z_ld, (a + 1) * 16)
                dve.wait_ge(oz_hi_ok, a)
                for m in range(2):
                    i = V.scalar_tensor_tensor(ozf[:, m], ps[:, OB, VD + m * P:VD + (m + 1) * P], sub8[:, m:m + 1],
                                               z_sb[:, m], ALU.mult, ALU.mult)
                i.then_inc(ozf_ok, 1)

            def oz_low(h, qb):
                a = h * NB + qb
                dve.wait_ge(oz_hi_ok, a + 1)
                if isinstance(h, int) and h == HEADS - 1:
                    kts, tok = slice(KT - 2, KT), slice(qb * P, (qb + 1) * P)
                    V.tensor_tensor(hT_lo[:, kts, tok], ozf[:, :, :], hT_hi[:, kts, tok].bitcast(F32),
                                    ALU.subtract).then_inc(oz7_ok, 1)
                else:
                    V.tensor_tensor(oz[:, 1], ozf[:, :, :], oz[:, 0].bitcast(F32), ALU.subtract).then_inc(oz_ok, 1)

            def combine(h, qb):
                a = h * NB + qb
                n = (qb + 1) * P
                dve.wait_ge(exp_done, a * 2 + 2)
                V.reciprocal(rinv[:, :], lsum[:, :]).then_inc(rinv_ok, 1)
                dve.wait_ge(rinv_ok, a + 1)
                V.scalar_tensor_tensor(coef[:, :], lsum[:, 0:1], lam[:, 3:4], rinv[:, 1:2], ALU.mult, ALU.mult).then_inc(coef_ok, 1)
                dve.wait_ge(coef_ok, a + 1)
                V.scalar_tensor_tensor(prob[:, 0, 0:n], prob[:, 1, 0:n], coef[:, 0:1], prob[:, 0, 0:n],
                                       ALU.mult, ALU.add).then_inc(comb_done, 1)

            def aT_low(h, qb):
                a = h * NB + qb
                dve.wait_ge(at_hi_ok, a + 1)
                V.tensor_tensor(aT_lo[:, 0:qb + 1], ps[:, SC:SC + 2].rearrange("p b (n c) -> p (b n) c", c=P)[:, 0:qb + 1],
                                aT_hi[:, 0:qb + 1].bitcast(F32), ALU.subtract).then_inc(at_done, 1)

            def step(h, cc, prev):
                G = h * COLS + cc
                ph, pc = (h, cc - 1) if cc else (h - 1, COLS - 1)
                last = (h - 1, cc - 1) if cc else (h - 2, NB - 1)
                split_w(G, 1)
                maxes(h - 1, cc, 0)
                if prev:
                    out_scale(*last)
                evict(ph, pc)
                split_w(G, 2)
                maxes(h - 1, cc, 1)
                if prev:
                    gate(*last)
                if pc // 2 == 2:
                    v_low(ph, pc, 0)
                combine(h - 1, cc)
                if prev:
                    oz_low(*last)
                split_w(G, 3)
                if pc // 2 == 2:
                    v_low(ph, pc, 1)
                split_w(G + 1, 0)
                aT_low(h - 1, cc)

            split_w(FIRST, 0)
            it = 0
            for cc in range(FIRST, COLS):
                for j in range(1, UNITS + 1):
                    if cc == FIRST and j == 1:
                        evict(0, 0)
                    split_w(cc + j // UNITS, j % UNITS)
                    if j == 1:
                        if cc == FIRST:
                            for c0 in range(1, FIRST):
                                evict(0, c0)
                        else:
                            evict(0, cc - 1)
                    if (cc - 1) // 2 == 2 and j in (2, 3):
                        v_low(0, cc - 1, j - 2)
                    if it < GCH * SUBS:
                        ada_rows((MCH * SUBS + it) * SR, (MCH * SUBS + it + 1) * SR)
                    if it % SUBS == 0 and it:
                        i = it // SUBS - 1
                        dve.wait_ge(mod_mm, MCH + i + 1)
                        k = 4 * i
                        V.tensor_tensor(mod[:, 2 * KT + k:2 * KT + k + 4], ps[:, OB, 0:4],
                                        cols[:, R_B + 2 * KT + k:R_B + 2 * KT + k + 4], ALU.add).then_inc(mod_ok, 1)
                    it += 1
            dve.wait_ge(mod_ok, MCH + GCH)
            V.tensor_tensor(mod[:, 2 * KT:3 * KT], mod[:, 2 * KT:3 * KT], cols[:, R_POST:R_POST + KT], ALU.mult).then_inc(gp_ok, 1)
            dve.wait_ge(gp_mm, 1)
            V.tensor_copy(gpT[0:KT, :], ps[0:KT, OB, 0:P]).then_inc(gp_cp, 1)

            for cc in range(COLS):
                step(1, cc, cc > 0)
            with dve.Fori(2, HEADS) as h:
                for cc in range(COLS):
                    step(h, cc, True)
            LH = HEADS - 1

            def y_scale(o):
                if o == 0:
                    dve.wait_ge(gpb_in, 16)
                ct = o % KT
                dve.wait_ge(yx_done, o + 1)
                if o < EARLY:
                    dst = yx[:, ct, HALF:SEQ].rearrange("p (t c) -> p t c", c=P)
                elif o < KT:
                    dst = y_sb[:, :, ct * P:(ct + 1) * P]
                else:
                    dst = yx[:, ct, 0:HALF].rearrange("p (t c) -> p t c", c=P)
                V.tensor_tensor(dst, ps[:, VX].rearrange("p (t c) -> p t c", c=P),
                                gpb[:, ct * P:(ct + 1) * P].rearrange("p (o c) -> p o c", o=1).to_broadcast([P, HT, P]),
                                ALU.mult).then_inc(y_ok, 1)

            def y_rms(half):
                dve.wait_ge(yss_ok, (half + 1) * KT * HT)
                V.tensor_reduce(out=yms[:, :], in_=yss[:, :, :], axis=AX.X, op=ALU.add).then_inc(yms_ok, 1)

            def finish(half, t):
                if t == 0:
                    dve.wait_ge(yrs_ok, half + 1)
                    dve.wait_ge(xh_in, (half + 1) * HT * 16)
                    dve.wait_ge(y_ok, (half + 1) * KT)
                if half:
                    tok = slice(t * P, (t + 1) * P)
                    y, r = yx[:, :, tok], x_late[:, :, tok]
                else:
                    y, r = y_sb[:, t], x_sb[:, t]
                V.scalar_tensor_tensor(r, y, yrs[:, t:t + 1], r, ALU.mult, ALU.add).then_inc(fin, 1)

            def tick(u):
                n = u + 1
                if n < len(OUT):
                    dve.wait_ge(w_hi_ok, U0 + n + 1)
                    V.tensor_tensor(w_lo[:, n % 2], w_raw[:, n % 4], w_hi[:, n % 2].bitcast(F32), ALU.subtract).then_inc(w_split, 1)
                for o in range(OT):
                    if END[o] == u - 3:
                        y_scale(o)
                if u == END[KT - 1] + 4:
                    y_rms(0)
                if 0 <= u - END[KT - 1] - 5 < HT:
                    finish(0, u - END[KT - 1] - 5)

            u = 0
            for qb in range(NB):
                n0, n1, n2 = SLOTS[qb]
                last = (LH, qb - 1) if qb else (LH - 1, NB - 1)
                maxes(LH, qb, 0)
                for i in range(n0):
                    tick(u + i)
                    if i == 0:
                        out_scale(*last)
                        if qb == 0:
                            evict(LH, COLS - 1)
                maxes(LH, qb, 1)
                for i in range(n1):
                    tick(u + n0 + i)
                    if i == 0:
                        gate(*last)
                        combine(LH, qb)
                        oz_low(*last)
                aT_low(LH, qb)
                for i in range(n2):
                    tick(u + n0 + n1 + i)
                u += n0 + n1 + n2
            tick(u)
            out_scale(LH, NB - 1)
            gate(LH, NB - 1)
            oz_low(LH, NB - 1)
            dve.wait_ge(y_ok, EARLY)
            V.tensor_copy(y_sb[:, :, 0:EARLY * P].rearrange("p t (k c) -> p k t c", c=P),
                          yx[:, 0:EARLY, HALF:SEQ].rearrange("p k (t c) -> p k t c", c=P)).then_inc(y_moved, 1)
            for v in range(u + 1, len(OUT) + 3):
                tick(v)
            y_rms(1)
            for t in range(HT):
                finish(1, t)

        @block.tensor
        def _(pe):
            MM, TR = nc.tensor.matmul, nc.tensor.transpose
            pe.wait_ge(consts, 8)
            pe.wait_ge(rows_in, 8 * 16)
            TR(ps[:, OB, 0:R_LAM + 4], rows[0:R_LAM + 4, :], ident[0:R_LAM + 4, 0:R_LAM + 4]).then_inc(cols_t, 1)
            pe.wait_ge(lam_p, 2)
            MM(ps[:, OB, P:P + 2], ones[:, :], lamp[:, :], start=True, stop=True).then_inc(lam_mm, 1)

            def mod_sum(ch):
                pe.wait_ge(acc_ok, (ch + 1) * TG)
                if ch:
                    pe.wait_ge(mod_ok, ch)
                else:
                    pe.wait_ge(lam_e, 1)
                for b in range(4):
                    dst, bc = ps[:, OB, b:b + 1], slice(b * P, (b + 1) * P)
                    for e in range(2):
                        i = MM(dst, acc[:, ch % 2, e, bc], ones[:, 0:1], start=e == 0, stop=e == 1)
                i.then_inc(mod_mm, 1)

            def x_tiles(k, half):
                n = 2 * k + half
                if n:
                    pe.wait_ge(h_ok, n)
                if k == 0:
                    pe.wait_ge(x_sc, (half + 1) * HT)
                for t in range(HT):
                    i = TR(ps[:, VX, t * P:(t + 1) * P], x_tok[:, k, half * HT + t], ident[:, :])
                i.then_inc(xT_mm, 1)

            def three(dst, a_hi, a_lo, b_hi, b_lo, start, stop):
                MM(dst, a_hi, b_hi, start=start, stop=False)
                MM(dst, a_hi, b_lo, start=False, stop=False)
                return MM(dst, a_lo, b_hi, start=False, stop=stop)

            mod_sum(0)
            x_tiles(0, 0)
            x_tiles(0, 1)
            for k in range(KT):
                i = k // 2
                if k % 2 == 0:
                    pe.wait_ge(w0_l, i + 1)
                elif i + 1 < MCH:
                    mod_sum(i + 1)
                pairs = [(half, cc) for half in range(2) for cc in range(FIRST)]
                if k == KT - 1:
                    pairs = [(half, cc) for cc in range(FIRST) for half in range(2)]
                for n, (half, cc) in enumerate(pairs):
                    tok = slice(half * HALF, (half + 1) * HALF)
                    wc = slice(cc * P, (cc + 1) * P)
                    pe.wait_ge(h_lo, 2 * k + half + 1)
                    last = three(ps[:, bank_of(0, cc, half)], w0_hi[:, i % 2, k % 2, wc], w0_lo[:, i % 2, k % 2, wc],
                                 hT_hi[:, k, tok], hT_lo[:, k, tok], k == 0, k == KT - 1)
                    if k == KT - 1:
                        last.then_inc(proj_done, 1)
                    elif n in (1, 4):
                        x_tiles(k + 1, n // 4)
                if k % 2 and i < MCH - 1:
                    last.then_inc(w0_used, 1)

            def unit(h, cc, j):
                G = h * COLS + cc
                n = unit_no(G, j)
                pe.wait_ge(w_split, n + 1)
                for half in range(2):
                    tok = slice(half * HALF, (half + 1) * HALF)
                    bank = bank_of(h, cc, half)
                    for kk in range(UK):
                        k = j * UK + kk
                        last = three(ps[:, bank], w_hi[:, j % 2, kk], w_lo[:, j % 2, kk], hT_hi[:, k, tok], hT_lo[:, k, tok],
                                     k == 0, k == KT - 1)
                    if j == UNITS - 1:
                        last.then_inc(proj_done, 1)
                if j < UNITS - 1:
                    last.then_inc(w_used, 1)

            def v_turn(h, cc, half):
                G = h * COLS + cc
                n = (cc % 2) * 2 + half
                pe.wait_ge(ev_done, G * 2 + half + 1)
                if not (isinstance(h, int) and h == 0 and n == 0):
                    pe.wait_ge(vt_done, h * 4 + n)
                for t in range(HT):
                    i = TR(ps[:, VX, t * P:(t + 1) * P], evf[:, half, t * P:(t + 1) * P], ident[:, :])
                i.then_inc(vt_mm, 1)

            def scores(h, qb, m):
                a = h * NB + qb
                if m == 0:
                    pe.wait_ge(q_ld, (a + 1) * 16)
                    pe.wait_ge(k_ld, (a + 1) * 16)
                    if not isinstance(a, int) or a > 0:
                        pe.wait_ge(at_done, a)
                else:
                    pe.wait_ge(exp_done, a * 2 + 1)
                n = (qb + 1) * P
                for b in range(0, n, HALF):
                    e = min(b + HALF, n)
                    dst = ps[:, SC + b // HALF, 0:e - b]
                    own = e == n
                    last = three(dst, q_sb[:, 2 * m], q_sb[:, 2 * m + 1], k_sb[:, 2 * m, b:e], k_sb[:, 2 * m + 1, b:e], True, not own)
                    if own:
                        last = MM(ps[:, SC + b // HALF, e - b - P:e - b], mcol[0:1, :], mrow[0:1, :], start=False, stop=True)
                last.then_inc(s_done, 1)

            def turn(h, qb):
                a = h * NB + qb
                pe.wait_ge(comb_done, a + 1)
                for b in range(qb + 1):
                    last = TR(ps[:, SC + b // HT, (b % HT) * P:(b % HT + 1) * P], prob[:, 0, b * P:(b + 1) * P], ident[:, :])
                last.then_inc(t_done, 1)

            def weighted(h, qb):
                a = h * NB + qb
                pe.wait_ge(at_done, a + 1)
                pe.wait_ge(v_ld, (a + 1) * 16)
                pe.wait_ge(ozf_ok, a)
                for b in range(qb + 1):
                    last = three(ps[:, OB, 0:VD], aT_hi[:, b], aT_lo[:, b], v_sb[:, b, 0], v_sb[:, b, 1], b == 0, b == qb)
                last.then_inc(pv_done, 1)

            def o_turn(h, qb):
                a = h * NB + qb
                pe.wait_ge(o_ok, a + 1)
                for m in range(2):
                    last = TR(ps[:, OB, VD + m * P:VD + (m + 1) * P], o_sb[:, m * P:(m + 1) * P], ident[:, :])
                last.then_inc(oT_done, 1)

            def step(h, cc, prev):
                ph, pc = (h, cc - 1) if cc else (h - 1, COLS - 1)
                G = h * COLS + cc
                scores(h - 1, cc, 0)
                pe.wait_ge(ev_done, (G - 1) * 2)
                unit(h, cc, 0)
                scores(h - 1, cc, 1)
                if prev:
                    o_turn(*((h - 1, cc - 1) if cc else (h - 2, NB - 1)))
                if pc // 2 == 2:
                    v_turn(ph, pc, 0)
                unit(h, cc, 1)
                if pc // 2 == 2:
                    v_turn(ph, pc, 1)
                unit(h, cc, 2)
                turn(h - 1, cc)
                unit(h, cc, 3)
                weighted(h - 1, cc)

            g = 0
            for cc in range(FIRST, COLS):
                pe.wait_ge(ev_done, 2 if cc == FIRST else 2 * (cc - 1))
                for j in range(UNITS):
                    unit(0, cc, j)
                    if (cc - 1) // 2 == 2 and j in (0, 1):
                        v_turn(0, cc - 1, j)
                    g += 1
                    if g % SUBS == 0 and g <= GCH * SUBS:
                        mod_sum(MCH + g // SUBS - 1)
            pe.wait_ge(gp_ok, 1)
            TR(ps[0:KT, OB, 0:P], mod[:, 2 * KT:3 * KT], ident[:, :]).then_inc(gp_mm, 1)
            pe.wait_ge(gp_cp, 1)
            for cc in range(COLS):
                step(1, cc, cc > 0)
            with pe.Fori(2, HEADS) as h:
                for cc in range(COLS):
                    step(h, cc, True)
            LH = HEADS - 1

            def y_turn(o):
                pe.wait_ge(yT_ok, o + 1)
                if o:
                    pe.wait_ge(yss_ok, o * HT)
                else:
                    pe.wait_ge(vt_done, HEADS * 4)
                for t in range(HT):
                    i = TR(ps[:, VX, t * P:(t + 1) * P], yT[:, o % 2, t * P:(t + 1) * P], ident[:, :])
                i.then_inc(yx_done, 1)

            def tick(u):
                if u < len(OUT):
                    o, j = OUT[u]
                    half = o // KT
                    tok = slice(half * HALF, (half + 1) * HALF)
                    if j == 0:
                        if o < 4:
                            pe.wait_ge(ev_done, HEADS * COLS * 2 - (2 if o < 2 else 3 - o))
                        else:
                            pe.wait_ge(yT_ok, o - 3)
                    if o == half * KT:
                        pe.wait_ge(oz_ld[half * UNITS + j], 2 * 16)
                        if j == UNITS - 1:
                            pe.wait_ge(oz7_ok, (half + 1) * HT)
                    pe.wait_ge(w_split, U0 + u + 1)
                    for kk in range(UK):
                        k = j * UK + kk
                        last = three(ps[:, o % 4], w_hi[:, u % 2, kk], w_lo[:, u % 2, kk], hT_hi[:, k, tok], hT_lo[:, k, tok],
                                     k == 0, k == KT - 1)
                    last.then_inc(w_used, 1)
                for o in range(OT):
                    if END[o] == u - 2:
                        y_turn(o)

            u = 0
            for qb in range(NB):
                n0, n1, n2 = SLOTS[qb]
                scores(LH, qb, 0)
                for i in range(n0):
                    tick(u + i)
                scores(LH, qb, 1)
                o_turn(*((LH, qb - 1) if qb else (LH - 1, NB - 1)))
                for i in range(n1):
                    tick(u + n0 + i)
                turn(LH, qb)
                for i in range(n2):
                    tick(u + n0 + n1 + i)
                weighted(LH, qb)
                u += n0 + n1 + n2
            tick(u)
            o_turn(LH, NB - 1)
            for v in range(u + 1, len(OUT) + 3):
                tick(v)


_INS = ["x", "c", "ada_w", "ada_b", "norm_pre", "norm_post", "diff_w_in", "diff_w_out", "diff_lambda_q1",
        "diff_lambda_k1", "diff_lambda_q2", "diff_lambda_k2", "diff_subln"]


def kernel(**inputs):
    import numpy as _np
    import concourse.bacc as _bacc
    from concourse import mybir as _mybir
    from concourse.bass_utils import run_bass_kernel_spmd as _run

    nc = _bacc.Bacc("TRN2", target_bir_lowering=False, num_devices=1, dynamic_dma_scratch_size=1024)
    arrays, args = {}, []
    for name in _INS:
        a = _np.ascontiguousarray(inputs[name])
        arrays[f"in_{name}_dram"] = a
        args.append(nc.dram_tensor(f"in_{name}_dram", a.shape, _mybir.dt.from_np(a.dtype), kind="ExternalInput").ap())
    out = nc.dram_tensor("out_0_dram", inputs["x"].shape, _mybir.dt.float32, kind="ExternalOutput").ap()
    build(nc, *args, out)
    r = _run(nc, [arrays], core_ids=[0])
    return r.results[0]["out_0_dram"]
```

```python
from contextlib import ExitStack

import concourse.bass as bass
from concourse import mybir

F32 = mybir.dt.float32
F32R = mybir.dt.float32r
ALU = mybir.AluOpType
ACT = mybir.ActivationFunctionType
AX = mybir.AxisListType

P = 128
EPS = 1e-6
LAMBDA_INIT = 0.8 - 0.6
MASKED = -1e30
CHUNK = 64


def build(nc, x, c, ada_w, ada_b, norm_pre, norm_post, w_in, w_out, lq1, lk1, lq2, lk2, subln, out):
    _, SEQ, D = x.shape
    VD = subln.shape[0]
    HEADS = D // VD
    KT = D // P
    TT = SEQ // P
    HALF = SEQ // 2
    HT = HALF // P
    UK = 4
    UNITS = KT // UK
    COLS = 8
    FIRST = 3
    QKSCALE = float(lq1.shape[0]) ** -0.5
    TG = D // P
    AC = 512
    SUBS = 4
    SR = TG // SUBS
    MCH = 2 * D // AC
    GCH = D // AC
    NB = SEQ // P
    AHEAD = 4

    GC = HALF
    GROUPS = D // GC
    OUTS = 2 * GROUPS * KT
    END = [(G + 1) * KT - 1 for G in range(2 * GROUPS)]
    SLOTS = [(1, 1, 1), (1, 1, 1), (1, 1, 1), (1, 1, 1), (1, 1, 2), (2, 2, 2), (2, 2, 2), (2, 2, 2)]
    assert sum(map(sum, SLOTS[:HT])) + SLOTS[HT][0] < KT - 2
    PARTS = 2
    EARLY = 2
    assert END[EARLY] >= sum(map(sum, SLOTS)) > END[EARLY - 1]

    ctx = ExitStack()
    with ctx:
        def sem(name):
            return ctx.enter_context(nc.semaphore(name))

        base = [nc.sbuf_base]

        def at(name, shape, dt, where=None):
            size = 4
            for n in shape[1:]:
                size *= n
            off = base[0] if where is None else where[0]
            off = (off + 31) // 32 * 32
            t = nc.alloc_sbuf_tensor_at(name, shape, dt, offset=off)
            (base if where is None else where)[0] = off + size
            return t

        hT_base = (base[0] + 31) // 32 * 32
        hT_hi_at = [hT_base]
        hT_hi = at("hT_hi", [P, KT, SEQ], F32R)
        hT_lo = at("hT_lo", [P, KT, SEQ], F32R)
        x_tok = at("x_tok", [P, KT, TT, P], F32, hT_hi_at)

        ident = at("ident", [P, P], F32)
        mhalf = at("mhalf", [P, TT], F32)
        w0_raw = at("w0_raw", [P, 2, 2, FIRST * P], F32, [base[0]])
        w_raw = at("w_raw", [P, 4, UK, P], F32)
        w_hi = at("w_hi", [P, 2, UK, P], F32R)
        w_lo = at("w_lo", [P, 2, UK, P], F32R)
        e_at = [base[0]]
        ev = at("ev", [P, 2, 2, HALF], F32R)
        evf = at("evf", [P, 2, HALF], F32)
        gpb = at("gpb", [P, D], F32, e_at)
        ysq = at("ysq", [P, GC], F32, e_at)
        yss = at("yss", [P, HT, GROUPS], F32)
        yms = at("yms", [P, HT], F32)
        yrs = at("yrs", [P, HT], F32)
        assert e_at[0] <= base[0]
        e_at = [base[0]]
        ones = at("ones", [P, P], F32)
        rows = at("rows", [P, P], F32)
        cols = at("cols", [P, P], F32)
        inv_vd = at("inv_vd", [P, 1], F32)
        eps_c = at("eps_c", [P, 1], F32)
        craw = at("craw", [P, TG], F32)
        cexp = at("cexp", [P, TG], F32)
        cact = at("cact", [P, TG], F32)
        mod = at("mod", [P, 3 * KT], F32)
        gpT = at("gpT", [P, P], F32)
        sub8 = at("sub8", [P, 2], F32)
        lamp = at("lamp", [P, 2], F32)
        lam = at("lam", [P, 4], F32)
        mcol = at("mcol", [P, P], F32R)
        mrow = at("mrow", [P, P], F32R)
        ssx = at("ssx", [P, TT], F32)
        rsx = at("rsx", [P, TT], F32)
        region = base[0]

        s_at = [region]
        ada = at("ada", [P, 4, SR, AC], F32, s_at)
        acc = at("acc", [P, 2, 2, AC], F32, s_at)
        ev0_at = [s_at[0]]
        w0_hi = at("w0_hi", [P, 2, 2, FIRST * P], F32R, s_at)
        w0_lo = at("w0_lo", [P, 2, 2, FIRST * P], F32R, s_at)
        h32 = at("h32", [P, 2, SEQ], F32, s_at)
        ev0 = at("ev0", [P, FIRST - 1, 2, 2, HALF], F32R, ev0_at)
        assert ev0_at[0] <= s_at[0]

        a_at = [region]
        k_sb = at("k_sb", [P, 4, SEQ], F32R, a_at)
        v_sb = at("v_sb", [P, TT, 2, VD], F32R, a_at)
        q_sb = at("q_sb", [P, 4, P], F32R, a_at)
        z_sb = at("z_sb", [P, 2, P], F32, a_at)
        prob = at("prob", [P, 2, SEQ], F32, a_at)
        aT_hi = at("aT_hi", [P, NB, P], F32R, a_at)
        aT_lo = at("aT_lo", [P, NB, P], F32R, a_at)
        o_sb = at("o_sb", [P, VD], F32, a_at)
        osq = at("osq", [P, VD], F32, a_at)
        ozf = at("ozf", [P, 2, P], F32, a_at)
        oz = at("oz", [P, 2, 2, P], F32R, a_at)
        nmax = at("nmax", [P, 2], F32, a_at)
        lsum = at("lsum", [P, 2], F32, a_at)
        rinv = at("rinv", [P, 2], F32, a_at)
        coef = at("coef", [P, 1], F32, a_at)
        oss = at("oss", [P, 1], F32, a_at)
        oms = at("oms", [P, 1], F32, a_at)
        orr = at("orr", [P, 1], F32, a_at)
        ofac = at("ofac", [P, 1], F32, a_at)

        y_sb = at("y_sb", [P, HT, D], F32, e_at)
        x_sb = at("x_sb", [P, HT, D], F32, e_at)
        hT_lo_at = [hT_hi_at[0]]
        yx = at("yx", [P, KT, SEQ], F32, hT_lo_at)
        x_late = at("x_late", [P, KT, SEQ], F32, [hT_base])
        for used in (s_at, a_at, e_at):
            assert used[0] <= nc.sbuf_usable_end, (used[0], nc.sbuf_usable_end)

        ps = ctx.enter_context(nc.psum_tensor("ps", [P, 8, HALF], F32))
        SC, VX, OB = 4, 6, 7

        def dram(name, shape):
            return nc.dram_tensor(name, shape, F32, kind="Internal").ap()

        q_dr = dram("q_dr", [HEADS * 4, P, SEQ])
        k_dr = dram("k_dr", [HEADS * 4, P, SEQ])
        v_dr = dram("v_dr", [HEADS * SEQ, 2, VD])
        z_dr = dram("z_dr", [HEADS * 2, P, SEQ])
        oz_dr = dram("oz_dr", [2, KT, P, SEQ])
        gp_dr = dram("gp_dr", [KT, P])

        rows_in, c_in = sem("rows_in"), sem("c_in")
        x_in = [sem(f"x_in{i}") for i in range(TT)]
        ada_in = [sem(f"ada_in{i}") for i in range(4)]
        w0_in = [sem(f"w0_in{i}") for i in range(2)]
        w_in_s = [sem(f"w_in{i}") for i in range(4)]
        consts = sem("consts")
        cols_t, cols_ok = sem("cols_t"), sem("cols_ok")
        lam_p, lam_mm, lam_e, lam_ok = sem("lam_p"), sem("lam_mm"), sem("lam_e"), sem("lam_ok")
        c_e, c_ok = sem("c_e"), sem("c_ok")
        x_sq, x_ms, x_rs, x_sc = sem("x_sq"), sem("x_ms"), sem("x_rs"), sem("x_sc")
        acc_ok, acc_used, mod_mm, mod_ok = sem("acc_ok"), sem("acc_used"), sem("mod_mm"), sem("mod_ok")
        mod_sum_ok = sem("mod_sum_ok")
        xT_mm, h_ok, h_hi, h_lo = sem("xT_mm"), sem("h_ok"), sem("h_hi"), sem("h_lo")
        w0_h, w0_l, w0_used = sem("w0_h"), sem("w0_l"), sem("w0_used")
        gp_ok, gp_mm, gp_cp, gp_st = sem("gp_ok"), sem("gp_mm"), sem("gp_cp"), sem("gp_st")
        w_hi_ok, w_split, w_used = sem("w_hi_ok"), sem("w_split"), sem("w_used")
        proj_done, ev_hi_ok, ev_done = sem("proj_done"), sem("ev_hi_ok"), sem("ev_done")
        oz7_ok, y_moved = sem("oz7_ok"), sem("y_moved")
        vt_mm, vt_hi, vt_done = sem("vt_mm"), sem("vt_hi"), sem("vt_done")
        stored = [sem("stored0"), sem("stored1")]
        q_ld, k_ld, v_ld, z_ld = sem("q_ld"), sem("k_ld"), sem("v_ld"), sem("z_ld")
        s_done, max_done, exp_done = sem("s_done"), sem("max_done"), sem("exp_done")
        rinv_ok, coef_ok, comb_done = sem("rinv_ok"), sem("coef_ok"), sem("comb_done")
        t_done, at_hi_ok, at_done = sem("t_done"), sem("at_hi_ok"), sem("at_done")
        pv_done, sq_done, fac_ok, o_ok = sem("pv_done"), sem("sq_done"), sem("fac_ok"), sem("o_ok")
        pl_mean, pl_ms, pl_rs = sem("pl_mean"), sem("pl_ms"), sem("pl_rs")
        oT_done, ozf_ok, oz_hi_ok, oz_ok, oz_st = (sem("oT_done"), sem("ozf_ok"), sem("oz_hi_ok"),
                                                   sem("oz_ok"), sem("oz_st"))
        oz_ld = [sem(f"oz_ld{i}") for i in range(2 * UNITS)]
        gpb_in, xh_in = sem("gpb_in"), sem("xh_in")
        out_done, y_ok, yss_ok = sem("out_done"), sem("y_ok"), sem("yss_ok")
        yms_ok, yr1, yrs_ok, fin, out_st = sem("yms_ok"), sem("yr1"), sem("yrs_ok"), sem("fin"), sem("out_st")

        ada_v = ada_w[0].rearrange("(p t) n -> p t n", t=TG)
        w_in_v = w_in.rearrange("(k p) n -> p k n", p=P)
        x_v = x[0].rearrange("(t p) (k c) -> p t k c", p=P, c=P)
        R_B, R_PRE, R_POST, R_SUB, R_LAM = 0, 3 * KT, 4 * KT, 5 * KT, 5 * KT + 2

        def unit_no(G, j):
            return (G - FIRST) * UNITS + j

        U0 = unit_no(HEADS * COLS, 0)
        USED0 = (HEADS * COLS - FIRST) * (UNITS - 1)

        def bank_of(h, cc, half):
            if isinstance(h, int) and h == 0 and cc < FIRST:
                return (2, 0, 4)[cc] + half
            return cc % 2 * 2 + half

        def bank_done(G, t):
            return (out_done, G * (HT - 1) + t + 1) if t < HT - 1 else (w_used, USED0 + END[G] + 1)

        block = ctx.enter_context(nc.Block())

        @block.sync
        def _(sp):
            def load_ada(s):
                ch, r = s // SUBS, s % SUBS
                if ch:
                    sp.wait_ge(acc_ok, (ch - 1) * TG + (r + 1) * SR)
                src = ada_v[:, r * SR:(r + 1) * SR]
                if ch < MCH:
                    src = src.rearrange("p t (m n) -> p t m n", m=3)[:, :, 0:2, ch * 256:(ch + 1) * 256]
                    dst = ada[:, r].rearrange("p t (m n) -> p t m n", m=2)
                    for m in range(2):
                        sp.dma_start(dst[:, :, m], src[:, :, m]).then_inc(ada_in[r], 16)
                else:
                    g = 2 * D + (ch - MCH) * AC
                    sp.dma_start(ada[:, r], src[:, :, g:g + AC]).then_inc(ada_in[r], 16)

            def load_w0(i):
                if i >= 2:
                    sp.wait_ge(w0_l, i - 1)
                sp.dma_start(w0_raw[:, i % 2, :, 0:VD], w_in_v[:, 2 * i:2 * i + 2, 0:VD]).then_inc(w0_in[i % 2], 16)
                sp.dma_start(w0_raw[:, i % 2, :, VD:FIRST * P],
                             w_in_v[:, 2 * i:2 * i + 2, D:D + FIRST * P - VD]).then_inc(w0_in[i % 2], 16)

            def w_cols(h, cc):
                part, m = cc // 2, cc % 2
                return bass.ds(h * VD + (part * D + m * P), P)

            def load_w(h, cc, j):
                n = unit_no(h * COLS + cc, j)
                if not isinstance(n, int) or n >= 4:
                    sp.wait_ge(w_split, n - 3)
                sp.dma_start(w_raw[:, j], w_in_v[:, j * UK:(j + 1) * UK, w_cols(h, cc)]).then_inc(w_in_s[j], 16)

            def store(h, cc, half):
                G, part, m = h * COLS + cc, cc // 2, cc % 2
                tok = slice(half * HALF, (half + 1) * HALF)
                if part == 2:
                    sp.wait_ge(vt_done, h * 4 + (m * 2 + half + 1))
                    dst = v_dr[bass.ds(h * SEQ + half * HALF, HALF)].rearrange("(t p) s d -> p t s d", p=P)
                    src = ev[:, half].rearrange("p s (t d) -> p t s d", t=HT).bitcast(F32)
                    for s in range(2):
                        last = sp.dma_start(dst[:, :, s, m * P:(m + 1) * P], src[:, :, s])
                        last.then_inc(stored[half], 16)
                    return
                sp.wait_ge(ev_done, G * 2 + half + 1)
                src = ev0[:, cc - 1, half] if isinstance(h, int) and h == 0 and 0 < cc < FIRST else ev[:, half]
                if part == 3:
                    sp.dma_start(z_dr[bass.ds(h * 2 + m, 1), :, tok].rearrange("h p n -> p h n"),
                                 evf[:, half:half + 1]).then_inc(stored[half], 32)
                else:
                    dr = (q_dr, k_dr)[part]
                    sp.dma_start(dr[bass.ds(h * 4 + m * 2, 2), :, tok].rearrange("s p n -> p s n"),
                                 src.bitcast(F32)).then_inc(stored[half], 32)

            def load_qk(h, qb):
                a = h * NB + qb
                if qb == 0:
                    for half in range(2):
                        sp.wait_ge(stored[half], (h * COLS + 4) * 32)
                if not isinstance(a, int) or a > 0:
                    sp.wait_ge(s_done, a * 2)
                tok = slice(qb * P, (qb + 1) * P)
                hd = bass.ds(h * 4, 4)
                sp.dma_start(q_sb[:, :, :].bitcast(F32), q_dr[hd, :, tok].rearrange("s p n -> p s n")).then_inc(q_ld, 16)
                sp.dma_start(k_sb[:, :, tok].bitcast(F32), k_dr[hd, :, tok].rearrange("s p n -> p s n")).then_inc(k_ld, 16)

            def load_v(h, qb):
                a = h * NB + qb
                if qb == 0:
                    for half in range(2):
                        sp.wait_ge(stored[half], (h * COLS + 6) * 32)
                sp.wait_ge(pv_done, a)
                sp.dma_start(v_sb[:, qb].bitcast(F32),
                             v_dr[bass.ds(h * SEQ + qb * P, P)]).then_inc(v_ld, 16)

            def load_z(h, qb):
                a = h * NB + qb
                if qb == 0:
                    for half in range(2):
                        sp.wait_ge(stored[half], (h * COLS + 8) * 32)
                sp.wait_ge(ozf_ok, a)
                sp.dma_start(z_sb[:, :, :],
                             z_dr[bass.ds(h * 2, 2), :, qb * P:(qb + 1) * P].rearrange("m p n -> p m n")).then_inc(z_ld, 16)

            def store_oz(h, qb):
                a = h * NB + qb
                sp.wait_ge(oz_ok, a + 1)
                for s in range(2):
                    sp.dma_start(oz_dr[s, bass.ds(h * 2, 2), :, qb * P:(qb + 1) * P].rearrange("m p n -> p m n"),
                                 oz[:, s].bitcast(F32)).then_inc(oz_st, 16)

            def head_steps(h, first):
                for cc in range(COLS):
                    nh, ncc = (h, cc + 1) if cc + 1 < COLS else (h + 1, 0)
                    pos = (h - 1, cc)
                    load_w(nh, ncc, 0)
                    load_v(*pos)
                    load_w(nh, ncc, 1)
                    load_w(nh, ncc, 2)
                    if not (first and cc == 0):
                        store_oz(*((h - 1, cc - 1) if cc else (h - 2, NB - 1)))
                    for half in range(2):
                        store(*((h, cc - 1) if cc else (h - 1, COLS - 1)), half)
                    load_w(nh, ncc, 3)
                    load_z(*pos)
                    load_qk(*((h - 1, cc + 1) if cc + 1 < NB else (h, 0)))

            for r in range(SUBS):
                load_ada(r)
            for t in range(TT):
                sp.dma_start(x_tok[:, :, t, :], x_v[:, t]).then_inc(x_in[t], 16)
            load_w0(0)
            for i in range(1, MCH):
                for r in range(SUBS):
                    load_ada(i * SUBS + r)
                    if r == 1:
                        load_w0(i)
            sp.wait_ge(w0_l, MCH)
            for j in range(UNITS):
                load_w(0, FIRST, j)
            g = 0
            for cc in range(FIRST, COLS):
                for j in range(UNITS):
                    if g < GCH * SUBS:
                        load_ada(MCH * SUBS + g)
                        g += 1
                    if cc + 1 < COLS:
                        load_w(0, cc + 1, j)
                    else:
                        load_w(1, 0, j)
                    if j == 1 and cc == FIRST:
                        for c0 in range(FIRST):
                            for half in range(2):
                                store(0, c0, half)
                    if j == 2 and cc > FIRST:
                        for half in range(2):
                            store(0, cc - 1, half)
            load_qk(0, 0)
            sp.wait_ge(gp_cp, 1)
            sp.dma_start(gp_dr[:, :], gpT[0:KT, :]).then_inc(gp_st, 16)

            head_steps(1, True)
            with sp.Fori(2, HEADS - 1) as h:
                head_steps(h, False)
            LH = HEADS - 1

            def load_wo(u):
                if u < OUTS:
                    g, k = u // KT % GROUPS, u % KT
                    sp.wait_ge(w_split, U0 + u - 3)
                    sp.dma_start(w_raw[:, u % 4],
                                 w_out[k * P:(k + 1) * P, g * GC:(g + 1) * GC].rearrange("p (a c) -> p a c", c=P),
                                 ).then_inc(w_in_s[u % 4], 16)

            def load_oz(half, s, j):
                tok = slice(half * HALF, (half + 1) * HALF)
                kts = slice(j * UK, min((j + 1) * UK, KT - 2))
                sp.dma_start((hT_hi, hT_lo)[s][:, kts, tok].bitcast(F32),
                             oz_dr[s, kts, :, tok].rearrange("k p n -> p k n")).then_inc(oz_ld[half * UNITS + j], 16)

            def load_oz_first(j):
                if j < UNITS - 1:
                    sp.wait_ge(w_used, USED0 - (UNITS - 2) + j)
                else:
                    sp.wait_ge(proj_done, HEADS * COLS * 2)
                if j == 0:
                    sp.wait_ge(oz_st, ((LH - 1) * NB + HT) * 32)
                load_oz(0, 0, j)
                load_oz(0, 1, j)

            for cc in range(COLS):
                def nxt(j):
                    if cc + 1 < COLS:
                        load_w(LH, cc + 1, j)
                    else:
                        load_wo(j)
                nxt(0)
                load_v(LH - 1, cc)
                nxt(1)
                nxt(2)
                if cc == COLS - 1:
                    load_oz_first(0)
                store_oz(*((LH - 1, cc - 1) if cc else (LH - 2, NB - 1)))
                for half in range(2):
                    store(*((LH, cc - 1) if cc else (LH - 1, COLS - 1)), half)
                nxt(3)
                load_z(LH - 1, cc)
                load_qk(*((LH - 1, cc + 1) if cc + 1 < NB else (LH, 0)))
            load_oz_first(1)

            u = 4
            for qb in range(NB):
                load_v(LH, qb)
                for i in range(3):
                    for _ in range(SLOTS[qb][i]):
                        load_wo(u)
                        u += 1
                    if i == 0:
                        if qb == 0:
                            for half in range(2):
                                store(LH, COLS - 1, half)
                        if qb in (1, 2):
                            load_oz_first(qb + 1)
                        if qb >= NB - UNITS:
                            sp.wait_ge(oz_st, LH * NB * 32)
                            load_oz(1, 0, qb - NB + UNITS)
                        if qb == 3:
                            for half in range(2):
                                sp.wait_ge(stored[half], HEADS * COLS * 32)
                            sp.wait_ge(gp_st, 16)
                            sp.dma_start(gpb[:, :], gp_dr.rearrange("k p -> (k p)")[None, :].to_broadcast([P, D])).then_inc(gpb_in, 16)
                    if i == 1:
                        if qb == 0:
                            store_oz(LH - 1, NB - 1)
                        load_z(LH, qb)
                        if qb + 1 < NB:
                            load_qk(LH, qb + 1)

            def load_x(half, t):
                r = (half * HT + t) * P
                if half:
                    sp.dma_start(x_late[:, :, t * P:(t + 1) * P],
                                 x[0, r:r + P, :].rearrange("p (k c) -> p k c", c=P)).then_inc(xh_in, 16)
                else:
                    sp.dma_start(x_sb[:, t], x[0, r:r + P, :]).then_inc(xh_in, 16)

            def store_out(half, t):
                r = (half * HT + t) * P
                if half:
                    for e in range(PARTS):
                        sp.wait_ge(fin, HT + t * PARTS + e + 1)
                        kts = slice(e * KT // PARTS, (e + 1) * KT // PARTS)
                        sp.dma_start(out[0, r:r + P, kts.start * P:kts.stop * P].rearrange("p (k c) -> p k c", c=P),
                                     x_late[:, kts, t * P:(t + 1) * P]).then_inc(out_st, 16)
                else:
                    sp.wait_ge(fin, t + 1)
                    sp.dma_start(out[0, r:r + P, :], x_sb[:, t]).then_inc(out_st, 16)

            moved = u - 4
            last0 = END[GROUPS - 1]
            for u in range(moved, OUTS):
                load_wo(u + 4)
                e = (u - moved - 3) // 2
                if (u - moved - 3) % 2 == 0 and 0 <= e < UNITS + HT:
                    if e == 0:
                        sp.wait_ge(y_moved, HT)
                        sp.wait_ge(oz7_ok, NB)
                    if e < UNITS:
                        load_oz(1, 1, e)
                    else:
                        load_x(0, e - UNITS)
                e = (u - last0 - 3) // 2
                if (u - last0 - 3) % 2 == 0 and 0 <= e < 2 * HT:
                    if e == 0:
                        sp.wait_ge(w_used, USED0 + last0 + 1)
                    if e < HT:
                        load_x(1, e)
                    else:
                        store_out(0, e - HT)
            for t in range(HT):
                store_out(1, t)
            sp.wait_ge(out_st, (HT + HT * PARTS) * 16)

        @block.gpsimd
        def _(pool):
            nc.gpsimd.memset(ones[:, :], 1.0).then_inc(consts, 1)
            nc.gpsimd.memset(ident[:, :], 0.0).then_inc(consts, 1)
            pool.wait_ge(consts, 2)
            nc.gpsimd.affine_select(out=ident[:, :], in_=ident[:, :], compare_op=ALU.not_equal, fill=1.0,
                                    base=0, pattern=[[-1, P]], channel_multiplier=1).then_inc(consts, 1)
            nc.gpsimd.memset(mhalf[:, :], -0.5).then_inc(consts, 1)
            nc.gpsimd.memset(mcol[0:1, :].bitcast(F32), 0.0).then_inc(consts, 1)
            nc.gpsimd.memset(mrow[0:1, :].bitcast(F32), 0.0).then_inc(consts, 1)
            pool.wait_ge(consts, 6)
            nc.gpsimd.memset(mcol[0:1, 0:CHUNK].bitcast(F32), 1.0).then_inc(consts, 1)
            nc.gpsimd.memset(mrow[0:1, CHUNK:P].bitcast(F32), MASKED).then_inc(consts, 1)
            nc.gpsimd.memset(inv_vd[:, :], 1.0 / VD).then_inc(consts, 1)
            nc.gpsimd.memset(eps_c[:, :], EPS).then_inc(consts, 1)
            pool.wait_ge(consts, 10)
            for t in range(TT):
                col = slice(t, t + 1)
                pool.wait_ge(x_sq, t + 1)
                nc.gpsimd.tensor_scalar(rsx[:, col], ssx[:, col], 1.0 / D, EPS, ALU.mult, ALU.add).then_inc(x_ms, 1)
                pool.wait_ge(x_ms, t + 1)
                nc.gpsimd.tensor_tensor(rsx[:, col], rsx[:, col], mhalf[:, col], ALU.pow).then_inc(x_rs, 1)

            def w0_low(i):
                pool.wait_ge(w0_h, i + 1)
                nc.gpsimd.tensor_tensor(w0_lo[:, i % 2], w0_raw[:, i % 2], w0_hi[:, i % 2].bitcast(F32),
                                        ALU.subtract).then_inc(w0_l, 1)

            w0_low(0)
            for k in range(KT):
                for half in range(2):
                    tok = slice(half * HALF, (half + 1) * HALF)
                    pool.wait_ge(h_hi, 2 * k + half + 1)
                    nc.gpsimd.tensor_tensor(hT_lo[:, k, tok], h32[:, k % 2, tok], hT_hi[:, k, tok].bitcast(F32),
                                            ALU.subtract).then_inc(h_lo, 1)
                if k % 2 and k + 1 < KT:
                    w0_low((k + 1) // 2)

            def out_factor(a):
                pool.wait_ge(sq_done, a + 1)
                nc.gpsimd.tensor_tensor(oms[:, :], oss[:, :], inv_vd[:, :], ALU.mult).then_inc(pl_mean, 1)
                pool.wait_ge(pl_mean, a + 1)
                nc.gpsimd.tensor_tensor(oms[:, :], oms[:, :], eps_c[:, :], ALU.add).then_inc(pl_ms, 1)
                pool.wait_ge(pl_ms, a + 1)
                nc.gpsimd.tensor_tensor(orr[:, :], oms[:, :], mhalf[:, 0:1], ALU.pow).then_inc(pl_rs, 1)
                pool.wait_ge(pl_rs, a + 1)
                if not isinstance(a, int) or a > 0:
                    pool.wait_ge(o_ok, a)
                nc.gpsimd.tensor_tensor(ofac[:, :], orr[:, :], rinv[:, 0:1], ALU.mult).then_inc(fac_ok, 1)

            out_factor(0)
            with pool.Fori(1, HEADS * NB) as a:
                out_factor(a)
            for half in range(2):
                pool.wait_ge(yms_ok, half + 1)
                nc.gpsimd.tensor_scalar(yrs[:, :], yms[:, :], 1.0 / D, EPS, ALU.mult, ALU.add).then_inc(yr1, 1)
                pool.wait_ge(yr1, half + 1)
                nc.gpsimd.tensor_tensor(yrs[:, :], yrs[:, :], mhalf[:, 0:HT], ALU.pow).then_inc(yrs_ok, 1)

        @block.scalar
        def _(act):
            A = nc.scalar.activation

            act.dma_start(craw[:, :], c[0].rearrange("(p t) -> p t", t=TG)).then_inc(c_in, 16)
            for lo, hi, v in ((R_B, R_PRE, ada_b[0]), (R_PRE, R_POST, norm_pre[0]), (R_POST, R_SUB, norm_post[0]),
                              (R_SUB, R_LAM, subln), (R_LAM, R_LAM + 1, lq1), (R_LAM + 1, R_LAM + 2, lk1),
                              (R_LAM + 2, R_LAM + 3, lq2), (R_LAM + 3, R_LAM + 4, lk2)):
                act.dma_start(rows[lo:hi, :], v.rearrange("(r p) -> r p", p=P)).then_inc(rows_in, 16)
            act.wait_ge(c_in, 16)
            A(cexp[:, :], craw[:, :], ACT.Exp, scale=-1.0).then_inc(c_e, 1)
            for t in range(TT):
                if t == 1:
                    act.wait_ge(lam_mm, 1)
                    A(lam[:, 0:2], ps[:, OB, P:P + 2], ACT.Exp).then_inc(lam_e, 1)
                act.wait_ge(x_in[t], 16)
                if t:
                    act.wait_ge(x_sq, t)
                A(h32[:, :, :].rearrange("p a (k c) -> p (a k) c", c=P), x_tok[:, :, t, :], ACT.Square,
                  accum_out=ssx[:, t:t + 1]).then_inc(x_sq, 1)
            act.wait_ge(x_sq, TT)

            def h_tile(k):
                act.wait_ge(mod_ok, k // 2 + 1)
                for half in range(2):
                    n = 2 * k + half
                    tok = slice(half * HALF, (half + 1) * HALF)
                    if k >= 2:
                        act.wait_ge(h_lo, n - 3)
                    act.wait_ge(xT_mm, n + 1)
                    A(h32[:, k % 2, tok], ps[:, VX], ACT.Identity,
                      scale=mod[:, KT + k:KT + k + 1], bias=mod[:, k:k + 1]).then_inc(h_ok, 1)
                    act.wait_ge(h_ok, n + 1)
                    A(hT_hi[:, k, tok], h32[:, k % 2, tok], ACT.Copy).then_inc(h_hi, 1)

            def w0_high(i):
                act.wait_ge(w0_in[i % 2], 32 * (i // 2 + 1))
                if i >= 2:
                    act.wait_ge(w0_used, i - 1)
                A(w0_hi[:, i % 2], w0_raw[:, i % 2], ACT.Copy).then_inc(w0_h, 1)

            w0_high(0)
            for k in range(KT):
                h_tile(k)
                if k % 2 and k + 1 < KT:
                    w0_high((k + 1) // 2)

            def split_w(G, j):
                n = unit_no(G, j)
                act.wait_ge(w_in_s[j], (G - FIRST + 1) * 16)
                if j == 1:
                    if not isinstance(G, int) or G > FIRST:
                        act.wait_ge(proj_done, G * 2)
                elif j >= 2 or not isinstance(G, int) or G > FIRST:
                    act.wait_ge(w_used, (G - FIRST) * (UNITS - 1) + (j - 1 if j >= 2 else 0))
                A(w_hi[:, j % 2], w_raw[:, j], ACT.Copy).then_inc(w_hi_ok, 1)

            def evict(h, cc):
                G, part = h * COLS + cc, cc // 2
                for half in range(2):
                    if part == 2:
                        continue
                    early = isinstance(h, int) and h == 0 and cc < FIRST
                    if early and cc:
                        act.wait_ge(proj_done, FIRST * 2)
                    elif early:
                        act.wait_ge(proj_done, half + 1)
                    else:
                        act.wait_ge(proj_done, G * 2 + half + 1)
                        act.wait_ge(stored[half], G * 32)
                    src = ps[:, bank_of(h, cc, half)]
                    if part == 3:
                        A(evf[:, half], src, ACT.Tanh, scale=0.5).then_inc(ev_hi_ok, 1)
                    else:
                        dst = ev0[:, cc - 1, half, 0] if early and cc else ev[:, half, 0]
                        A(dst, src, ACT.Copy, scale=QKSCALE if part == 0 else 1.0).then_inc(ev_hi_ok, 1)

            def v_high(h, cc, half):
                act.wait_ge(vt_mm, h * 4 + ((cc % 2) * 2 + half + 1))
                A(ev[:, half, 0], ps[:, VX], ACT.Copy).then_inc(vt_hi, 1)

            def exps(h, qb, m):
                a = h * NB + qb
                n = (qb + 1) * P
                act.wait_ge(max_done, a * 2 + m + 1)
                A(prob[:, m, 0:n], ps[:, SC:SC + 2].rearrange("p b n -> p (b n)")[:, 0:n], ACT.Exp,
                  bias=nmax[:, m:m + 1], accum_out=lsum[:, m:m + 1]).then_inc(exp_done, 1)

            def oz_high(h, qb):
                a = h * NB + qb
                act.wait_ge(ozf_ok, a + 1)
                if isinstance(h, int) and h == HEADS - 1:
                    dst = hT_hi[:, KT - 2:KT, qb * P:(qb + 1) * P]
                else:
                    dst = oz[:, 0]
                    act.wait_ge(oz_st, a * 32)
                A(dst, ozf[:, :, :], ACT.Copy).then_inc(oz_hi_ok, 1)

            def aT_high(h, qb):
                a = h * NB + qb
                act.wait_ge(t_done, a + 1)
                A(aT_hi[:, 0:qb + 1], ps[:, SC:SC + 2].rearrange("p b (n c) -> p (b n) c", c=P)[:, 0:qb + 1],
                  ACT.Copy).then_inc(at_hi_ok, 1)

            def square(h, qb):
                a = h * NB + qb
                act.wait_ge(pv_done, a + 1)
                if not isinstance(a, int) or a > 0:
                    act.wait_ge(pl_ms, a)
                    act.wait_ge(sq_done, a)
                A(osq[:, :], ps[:, OB, 0:VD], ACT.Square, scale=rinv[:, 0:1], accum_out=oss[:, :]).then_inc(sq_done, 1)

            def step(h, cc, prev_oz):
                G = h * COLS + cc
                ph, pc = (h, cc - 1) if cc else (h - 1, COLS - 1)
                split_w(G, 1)
                exps(h - 1, cc, 0)
                evict(ph, pc)
                split_w(G, 2)
                exps(h - 1, cc, 1)
                if pc // 2 == 2:
                    v_high(ph, pc, 0)
                if prev_oz:
                    oz_high(*((h - 1, cc - 1) if cc else (h - 2, NB - 1)))
                split_w(G, 3)
                if pc // 2 == 2:
                    v_high(ph, pc, 1)
                split_w(G + 1, 0)
                aT_high(h - 1, cc)
                square(h - 1, cc)

            split_w(FIRST, 0)
            for cc in range(FIRST, COLS):
                if cc == FIRST:
                    for c0 in range(FIRST):
                        evict(0, c0)
                        if c0 == 0:
                            split_w(cc, 1)
                else:
                    split_w(cc, 1)
                    evict(0, cc - 1)
                split_w(cc, 2)
                if (cc - 1) // 2 == 2:
                    v_high(0, cc - 1, 0)
                split_w(cc, 3)
                if (cc - 1) // 2 == 2:
                    v_high(0, cc - 1, 1)
                split_w(cc + 1, 0)
            for cc in range(COLS):
                step(1, cc, cc > 0)
            with act.Fori(2, HEADS) as h:
                for cc in range(COLS):
                    step(h, cc, True)
            LH = HEADS - 1

            def y_square(G, t):
                act.wait_ge(*bank_done(G, t))
                if G == 0 and t == 0:
                    for half in range(2):
                        act.wait_ge(stored[half], HEADS * COLS * 32)
                if G == GROUPS and t == 0:
                    act.wait_ge(yms_ok, 1)
                if G + t:
                    act.wait_ge(yss_ok, G * HT + t)
                A(ysq[:, :], ps[:, t], ACT.Square, accum_out=yss[:, t, G % GROUPS:G % GROUPS + 1]).then_inc(yss_ok, 1)

            def split_next(u):
                n = u + 1
                if n < OUTS:
                    act.wait_ge(w_in_s[n % 4], (HEADS * COLS - FIRST + n // 4 + 1) * 16)
                    if n == 1:
                        act.wait_ge(proj_done, HEADS * COLS * 2)
                    else:
                        act.wait_ge(w_used, USED0 + n - 1)
                    A(w_hi[:, n % 2], w_raw[:, n % 4], ACT.Copy).then_inc(w_hi_ok, 1)

            def tiles_done(u):
                if u in END:
                    for t in range(HT):
                        y_square(u // KT, t)

            u = 0
            for qb in range(NB):
                n0, n1, n2 = SLOTS[qb]
                split_next(u)
                if qb == 0:
                    evict(LH, COLS - 1)
                exps(LH, qb, 0)
                tiles_done(u)
                for i in range(1, n0):
                    split_next(u + i)
                    tiles_done(u + i)
                split_next(u + n0)
                exps(LH, qb, 1)
                oz_high(*((LH, qb - 1) if qb else (LH - 1, NB - 1)))
                tiles_done(u + n0)
                for i in range(1, n1):
                    split_next(u + n0 + i)
                    tiles_done(u + n0 + i)
                if n2:
                    split_next(u + n0 + n1)
                aT_high(LH, qb)
                for i in range(n2):
                    if i:
                        split_next(u + n0 + n1 + i)
                    tiles_done(u + n0 + n1 + i)
                square(LH, qb)
                u += n0 + n1 + n2
            split_next(u)
            split_next(u + 1)
            oz_high(LH, NB - 1)
            for v in range(u + 2, OUTS):
                split_next(v)
                tiles_done(v)

        @block.vector
        def _(dve):
            V = nc.vector
            def x_scale(t):
                dve.wait_ge(x_rs, t + 1)
                V.tensor_scalar(x_tok[:, :, t, :], x_tok[:, :, t, :], rsx[:, t:t + 1], None, ALU.mult).then_inc(x_sc, 1)

            dve.wait_ge(c_e, 1)
            V.tensor_scalar(cexp[:, :], cexp[:, :], 1.0, None, ALU.add).then_inc(c_ok, 1)
            dve.wait_ge(c_ok, 1)
            V.reciprocal(cexp[:, :], cexp[:, :]).then_inc(c_ok, 1)
            dve.wait_ge(c_ok, 2)
            V.tensor_tensor(cact[:, :], craw[:, :], cexp[:, :], ALU.mult).then_inc(c_ok, 1)
            dve.wait_ge(c_ok, 3)

            def ada_rows(lo, hi):
                for n in range(lo, hi):
                    ch, g = n // TG, n % TG
                    r, t = g // SR, g % SR
                    if t == 0:
                        loads = 2 * min(ch + 1, MCH) + max(ch + 1 - MCH, 0)
                        dve.wait_ge(ada_in[r], 16 * loads)
                    if g == 0 and ch >= 2:
                        dve.wait_ge(mod_mm, ch - 1)
                    dst, w = acc[:, ch % 2, g % 2], ada[:, r, t]
                    if g < 2:
                        i = V.tensor_scalar(dst, w, cact[:, g:g + 1], None, ALU.mult)
                    else:
                        dve.wait_ge(acc_ok, n - 1)
                        i = V.scalar_tensor_tensor(dst, w, cact[:, g:g + 1], dst, ALU.mult, ALU.add)
                    i.then_inc(acc_ok, 1)

            def mod_cols(i):
                dve.wait_ge(mod_mm, i + 1)
                k = 2 * i
                V.tensor_tensor(mod[:, k:k + 2], ps[:, OB, 0:2], cols[:, R_B + k:R_B + k + 2], ALU.add).then_inc(mod_sum_ok, 1)
                V.scalar_tensor_tensor(mod[:, KT + k:KT + k + 2], ps[:, OB, 2:4], 1.0,
                                       cols[:, R_B + KT + k:R_B + KT + k + 2], ALU.add, ALU.add).then_inc(mod_sum_ok, 1)
                dve.wait_ge(mod_sum_ok, 2 * i + 2)
                V.tensor_tensor(mod[:, KT + k:KT + k + 2], mod[:, KT + k:KT + k + 2],
                                cols[:, R_PRE + k:R_PRE + k + 2], ALU.mult).then_inc(mod_ok, 1)

            ada_rows(0, SR)
            dve.wait_ge(cols_t, 1)
            V.tensor_copy(cols[:, 0:R_LAM + 4], ps[:, OB, 0:R_LAM + 4]).then_inc(cols_ok, 1)
            dve.wait_ge(cols_ok, 1)
            V.tensor_tensor(lamp[:, 0:1], cols[:, R_LAM:R_LAM + 1], cols[:, R_LAM + 1:R_LAM + 2], ALU.mult).then_inc(lam_p, 1)
            V.tensor_tensor(lamp[:, 1:2], cols[:, R_LAM + 2:R_LAM + 3], cols[:, R_LAM + 3:R_LAM + 4], ALU.mult).then_inc(lam_p, 1)
            V.tensor_scalar(sub8[:, :], cols[:, R_SUB:R_SUB + 2], (1.0 - LAMBDA_INIT) / 2, None, ALU.mult).then_inc(cols_ok, 1)
            ada_rows(SR, TG)
            dve.wait_ge(lam_e, 1)
            V.tensor_tensor(lam[:, 2:3], lam[:, 1:2], lam[:, 0:1], ALU.subtract).then_inc(lam_ok, 1)
            dve.wait_ge(lam_ok, 1)
            V.tensor_scalar(lam[:, 3:4], lam[:, 2:3], -LAMBDA_INIT, None, ALU.add).then_inc(lam_ok, 1)
            for t in range(TT):
                x_scale(t)
                if t == 0:
                    mod_cols(0)
            for i in range(1, MCH):
                ada_rows(i * TG + (AHEAD if i > 1 else 0), (i + 1) * TG)
                if i + 1 < MCH:
                    ada_rows((i + 1) * TG, (i + 1) * TG + AHEAD)
                mod_cols(i)

            def split_w(G, j):
                n = unit_no(G, j)
                dve.wait_ge(w_hi_ok, n + 1)
                V.tensor_tensor(w_lo[:, j % 2], w_raw[:, j], w_hi[:, j % 2].bitcast(F32), ALU.subtract).then_inc(w_split, 1)

            def evict(h, cc):
                G, part = h * COLS + cc, cc // 2
                for half in range(2):
                    src = ps[:, bank_of(h, cc, half)]
                    buf = ev0[:, cc - 1, half] if isinstance(h, int) and h == 0 and 0 < cc < FIRST else ev[:, half]
                    if part == 2:
                        dve.wait_ge(proj_done, G * 2 + half + 1)
                        dve.wait_ge(stored[half], G * 32)
                        V.tensor_copy(evf[:, half], src).then_inc(ev_done, 1)
                        continue
                    n = {0: 0, 1: 4, 3: 8}[part] + (cc % 2) * 2 + half + 1
                    dve.wait_ge(ev_hi_ok, h * 12 + n)
                    if part == 3:
                        V.scalar_tensor_tensor(evf[:, half], evf[:, half], 1.0, src, ALU.add, ALU.mult).then_inc(ev_done, 1)
                    elif part == 0:
                        V.scalar_tensor_tensor(buf[:, 1], src, QKSCALE, buf[:, 0].bitcast(F32),
                                               ALU.mult, ALU.subtract).then_inc(ev_done, 1)
                    else:
                        V.tensor_tensor(buf[:, 1], src, buf[:, 0].bitcast(F32), ALU.subtract).then_inc(ev_done, 1)

            def v_low(h, cc, half):
                dve.wait_ge(vt_hi, h * 4 + ((cc % 2) * 2 + half + 1))
                V.tensor_tensor(ev[:, half, 1], ps[:, VX], ev[:, half, 0].bitcast(F32), ALU.subtract).then_inc(vt_done, 1)

            def maxes(h, qb, m):
                a = h * NB + qb
                n = (qb + 1) * P
                dve.wait_ge(s_done, a * 2 + m + 1)
                V.tensor_reduce(out=nmax[:, m:m + 1], in_=ps[:, SC:SC + 2].rearrange("p b n -> p (b n)")[:, 0:n],
                                axis=AX.X, op=ALU.max, negate=True).then_inc(max_done, 1)

            def out_scale(h, qb):
                a = h * NB + qb
                dve.wait_ge(fac_ok, a + 1)
                if not isinstance(a, int) or a > 0:
                    dve.wait_ge(oT_done, a)
                V.tensor_scalar(o_sb[:, :], ps[:, OB, 0:VD], ofac[:, 0:1], None, ALU.mult).then_inc(o_ok, 1)

            def gate(h, qb):
                a = h * NB + qb
                dve.wait_ge(oT_done, a + 1)
                dve.wait_ge(z_ld, (a + 1) * 16)
                dve.wait_ge(oz_hi_ok, a)
                for m in range(2):
                    i = V.scalar_tensor_tensor(ozf[:, m], ps[:, OB, VD + m * P:VD + (m + 1) * P], sub8[:, m:m + 1],
                                               z_sb[:, m], ALU.mult, ALU.mult)
                i.then_inc(ozf_ok, 1)

            def oz_low(h, qb):
                a = h * NB + qb
                dve.wait_ge(oz_hi_ok, a + 1)
                if isinstance(h, int) and h == HEADS - 1:
                    kts, tok = slice(KT - 2, KT), slice(qb * P, (qb + 1) * P)
                    V.tensor_tensor(hT_lo[:, kts, tok], ozf[:, :, :], hT_hi[:, kts, tok].bitcast(F32),
                                    ALU.subtract).then_inc(oz7_ok, 1)
                else:
                    V.tensor_tensor(oz[:, 1], ozf[:, :, :], oz[:, 0].bitcast(F32), ALU.subtract).then_inc(oz_ok, 1)

            def combine(h, qb):
                a = h * NB + qb
                n = (qb + 1) * P
                dve.wait_ge(exp_done, a * 2 + 2)
                V.reciprocal(rinv[:, :], lsum[:, :]).then_inc(rinv_ok, 1)
                dve.wait_ge(rinv_ok, a + 1)
                V.scalar_tensor_tensor(coef[:, :], lsum[:, 0:1], lam[:, 3:4], rinv[:, 1:2], ALU.mult, ALU.mult).then_inc(coef_ok, 1)
                dve.wait_ge(coef_ok, a + 1)
                V.scalar_tensor_tensor(prob[:, 0, 0:n], prob[:, 1, 0:n], coef[:, 0:1], prob[:, 0, 0:n],
                                       ALU.mult, ALU.add).then_inc(comb_done, 1)

            def aT_low(h, qb):
                a = h * NB + qb
                dve.wait_ge(at_hi_ok, a + 1)
                V.tensor_tensor(aT_lo[:, 0:qb + 1], ps[:, SC:SC + 2].rearrange("p b (n c) -> p (b n) c", c=P)[:, 0:qb + 1],
                                aT_hi[:, 0:qb + 1].bitcast(F32), ALU.subtract).then_inc(at_done, 1)

            def step(h, cc, prev):
                G = h * COLS + cc
                ph, pc = (h, cc - 1) if cc else (h - 1, COLS - 1)
                last = (h - 1, cc - 1) if cc else (h - 2, NB - 1)
                split_w(G, 1)
                maxes(h - 1, cc, 0)
                if prev:
                    out_scale(*last)
                evict(ph, pc)
                split_w(G, 2)
                maxes(h - 1, cc, 1)
                if prev:
                    gate(*last)
                if pc // 2 == 2:
                    v_low(ph, pc, 0)
                combine(h - 1, cc)
                if prev:
                    oz_low(*last)
                split_w(G, 3)
                if pc // 2 == 2:
                    v_low(ph, pc, 1)
                split_w(G + 1, 0)
                aT_low(h - 1, cc)

            split_w(FIRST, 0)
            it = 0
            for cc in range(FIRST, COLS):
                for j in range(1, UNITS + 1):
                    if cc == FIRST and j == 1:
                        evict(0, 0)
                    split_w(cc + j // UNITS, j % UNITS)
                    if j == 1:
                        if cc == FIRST:
                            for c0 in range(1, FIRST):
                                evict(0, c0)
                        else:
                            evict(0, cc - 1)
                    if (cc - 1) // 2 == 2 and j in (2, 3):
                        v_low(0, cc - 1, j - 2)
                    if it < GCH * SUBS:
                        ada_rows((MCH * SUBS + it) * SR, (MCH * SUBS + it + 1) * SR)
                    if it % SUBS == 0 and it:
                        i = it // SUBS - 1
                        dve.wait_ge(mod_mm, MCH + i + 1)
                        k = 4 * i
                        V.tensor_tensor(mod[:, 2 * KT + k:2 * KT + k + 4], ps[:, OB, 0:4],
                                        cols[:, R_B + 2 * KT + k:R_B + 2 * KT + k + 4], ALU.add).then_inc(mod_ok, 1)
                        if i == GCH - 1:
                            dve.wait_ge(mod_ok, MCH + GCH)
                            V.tensor_tensor(mod[:, 2 * KT:3 * KT], mod[:, 2 * KT:3 * KT], cols[:, R_POST:R_POST + KT],
                                            ALU.mult).then_inc(gp_ok, 1)
                    if it == GCH * SUBS + 2:
                        dve.wait_ge(gp_mm, 1)
                        V.tensor_copy(gpT[0:KT, :], ps[0:KT, OB, 0:P]).then_inc(gp_cp, 1)
                    it += 1

            for cc in range(COLS):
                step(1, cc, cc > 0)
            with dve.Fori(2, HEADS) as h:
                for cc in range(COLS):
                    step(h, cc, True)
            LH = HEADS - 1

            def y_scale(G, t):
                half, g = G // GROUPS, G % GROUPS
                if G == 0 and t == 0:
                    dve.wait_ge(gpb_in, 16)
                dve.wait_ge(yss_ok, G * HT + t + 1)
                kts, tok = slice(g * GC // P, (g + 1) * GC // P), slice(t * P, (t + 1) * P)
                if G < EARLY:
                    dst = yx[:, kts, HALF + t * P:HALF + (t + 1) * P]
                elif half == 0:
                    dst = y_sb[:, t, g * GC:(g + 1) * GC].rearrange("p (k c) -> p k c", c=P)
                else:
                    dst = yx[:, kts, tok]
                V.tensor_tensor(dst, ps[:, t].rearrange("p (k c) -> p k c", c=P),
                                gpb[:, g * GC:(g + 1) * GC].rearrange("p (k c) -> p k c", c=P), ALU.mult).then_inc(y_ok, 1)

            def y_rms(half):
                dve.wait_ge(yss_ok, (half + 1) * GROUPS * HT)
                V.tensor_reduce(out=yms[:, :], in_=yss[:, :, :], axis=AX.X, op=ALU.add).then_inc(yms_ok, 1)

            def finish(half, t):
                if t == 0:
                    dve.wait_ge(yrs_ok, half + 1)
                    dve.wait_ge(xh_in, (half + 1) * HT * 16)
                    dve.wait_ge(y_ok, (half + 1) * GROUPS * HT)
                if half:
                    tok = slice(t * P, (t + 1) * P)
                    for e in range(PARTS):
                        kts = slice(e * KT // PARTS, (e + 1) * KT // PARTS)
                        y, r = yx[:, kts, tok], x_late[:, kts, tok]
                        V.scalar_tensor_tensor(r, y, yrs[:, t:t + 1], r, ALU.mult, ALU.add).then_inc(fin, 1)
                else:
                    y, r = y_sb[:, t], x_sb[:, t]
                    V.scalar_tensor_tensor(r, y, yrs[:, t:t + 1], r, ALU.mult, ALU.add).then_inc(fin, 1)

            def split_next(u):
                n = u + 1
                if n < OUTS:
                    dve.wait_ge(w_hi_ok, U0 + n + 1)
                    V.tensor_tensor(w_lo[:, n % 2], w_raw[:, n % 4], w_hi[:, n % 2].bitcast(F32), ALU.subtract).then_inc(w_split, 1)

            def tiles_done(u):
                if u in END:
                    for t in range(HT):
                        y_scale(u // KT, t)
                if u == END[GROUPS - 1] + 1:
                    y_rms(0)
                if 0 <= u - END[GROUPS - 1] - 3 < HT:
                    finish(0, u - END[GROUPS - 1] - 3)

            u = 0
            for qb in range(NB):
                n0, n1, n2 = SLOTS[qb]
                last = (LH, qb - 1) if qb else (LH - 1, NB - 1)
                split_next(u)
                if qb == 0:
                    evict(LH, COLS - 1)
                maxes(LH, qb, 0)
                out_scale(*last)
                tiles_done(u)
                for i in range(1, n0):
                    split_next(u + i)
                    tiles_done(u + i)
                split_next(u + n0)
                maxes(LH, qb, 1)
                gate(*last)
                combine(LH, qb)
                oz_low(*last)
                tiles_done(u + n0)
                for i in range(1, n1):
                    split_next(u + n0 + i)
                    tiles_done(u + n0 + i)
                if n2:
                    split_next(u + n0 + n1)
                aT_low(LH, qb)
                for i in range(n2):
                    if i:
                        split_next(u + n0 + n1 + i)
                    tiles_done(u + n0 + n1 + i)
                u += n0 + n1 + n2
            split_next(u)
            split_next(u + 1)
            out_scale(LH, NB - 1)
            gate(LH, NB - 1)
            oz_low(LH, NB - 1)
            for v in range(u + 2, OUTS):
                split_next(v)
                if v < u + 2 + HT:
                    t, n = v - u - 2, EARLY * GC // P
                    dve.wait_ge(y_ok, EARLY * HT)
                    V.tensor_copy(y_sb[:, t, 0:n * P].rearrange("p (k c) -> p k c", c=P),
                                  yx[:, 0:n, HALF + t * P:HALF + (t + 1) * P]).then_inc(y_moved, 1)
                tiles_done(v)
            y_rms(1)
            for t in range(HT):
                finish(1, t)

        @block.tensor
        def _(pe):
            MM, TR = nc.tensor.matmul, nc.tensor.transpose
            pe.wait_ge(consts, 8)
            pe.wait_ge(rows_in, 8 * 16)
            TR(ps[:, OB, 0:R_LAM + 4], rows[0:R_LAM + 4, :], ident[0:R_LAM + 4, 0:R_LAM + 4]).then_inc(cols_t, 1)
            pe.wait_ge(lam_p, 2)
            MM(ps[:, OB, P:P + 2], ones[:, :], lamp[:, :], start=True, stop=True).then_inc(lam_mm, 1)

            def mod_sum(ch):
                pe.wait_ge(acc_ok, (ch + 1) * TG)
                if ch:
                    pe.wait_ge(mod_ok, ch)
                else:
                    pe.wait_ge(lam_e, 1)
                for b in range(4):
                    dst, bc = ps[:, OB, b:b + 1], slice(b * P, (b + 1) * P)
                    for e in range(2):
                        i = MM(dst, acc[:, ch % 2, e, bc], ones[:, 0:1], start=e == 0, stop=e == 1)
                i.then_inc(mod_mm, 1)

            def x_tiles(k, half):
                n = 2 * k + half
                if n:
                    pe.wait_ge(h_ok, n)
                if k == 0:
                    pe.wait_ge(x_sc, (half + 1) * HT)
                for t in range(HT):
                    i = TR(ps[:, VX, t * P:(t + 1) * P], x_tok[:, k, half * HT + t], ident[:, :])
                i.then_inc(xT_mm, 1)

            def three(dst, a_hi, a_lo, b_hi, b_lo, start, stop):
                MM(dst, a_hi, b_hi, start=start, stop=False)
                MM(dst, a_hi, b_lo, start=False, stop=False)
                return MM(dst, a_lo, b_hi, start=False, stop=stop)

            mod_sum(0)
            x_tiles(0, 0)
            x_tiles(0, 1)
            for k in range(KT):
                i = k // 2
                if k % 2 == 0:
                    pe.wait_ge(w0_l, i + 1)
                elif i + 1 < MCH:
                    mod_sum(i + 1)
                pairs = [(half, cc) for half in range(2) for cc in range(FIRST)]
                if k == KT - 1:
                    pairs = [(half, cc) for cc in range(FIRST) for half in range(2)]
                for n, (half, cc) in enumerate(pairs):
                    tok = slice(half * HALF, (half + 1) * HALF)
                    wc = slice(cc * P, (cc + 1) * P)
                    pe.wait_ge(h_lo, 2 * k + half + 1)
                    last = three(ps[:, bank_of(0, cc, half)], w0_hi[:, i % 2, k % 2, wc], w0_lo[:, i % 2, k % 2, wc],
                                 hT_hi[:, k, tok], hT_lo[:, k, tok], k == 0, k == KT - 1)
                    if k == KT - 1:
                        last.then_inc(proj_done, 1)
                    elif n in (1, 4):
                        x_tiles(k + 1, n // 4)
                if k % 2 and i < MCH - 1:
                    last.then_inc(w0_used, 1)

            def unit(h, cc, j):
                G = h * COLS + cc
                n = unit_no(G, j)
                pe.wait_ge(w_split, n + 1)
                for half in range(2):
                    tok = slice(half * HALF, (half + 1) * HALF)
                    bank = bank_of(h, cc, half)
                    for kk in range(UK):
                        k = j * UK + kk
                        last = three(ps[:, bank], w_hi[:, j % 2, kk], w_lo[:, j % 2, kk], hT_hi[:, k, tok], hT_lo[:, k, tok],
                                     k == 0, k == KT - 1)
                    if j == UNITS - 1:
                        last.then_inc(proj_done, 1)
                if j < UNITS - 1:
                    last.then_inc(w_used, 1)

            def v_turn(h, cc, half):
                G = h * COLS + cc
                n = (cc % 2) * 2 + half
                pe.wait_ge(ev_done, G * 2 + half + 1)
                if not (isinstance(h, int) and h == 0 and n == 0):
                    pe.wait_ge(vt_done, h * 4 + n)
                for t in range(HT):
                    i = TR(ps[:, VX, t * P:(t + 1) * P], evf[:, half, t * P:(t + 1) * P], ident[:, :])
                i.then_inc(vt_mm, 1)

            def scores(h, qb, m):
                a = h * NB + qb
                if m == 0:
                    pe.wait_ge(q_ld, (a + 1) * 16)
                    pe.wait_ge(k_ld, (a + 1) * 16)
                    if not isinstance(a, int) or a > 0:
                        pe.wait_ge(at_done, a)
                else:
                    pe.wait_ge(exp_done, a * 2 + 1)
                n = (qb + 1) * P
                for b in range(0, n, HALF):
                    e = min(b + HALF, n)
                    dst = ps[:, SC + b // HALF, 0:e - b]
                    own = e == n
                    last = three(dst, q_sb[:, 2 * m], q_sb[:, 2 * m + 1], k_sb[:, 2 * m, b:e], k_sb[:, 2 * m + 1, b:e], True, not own)
                    if own:
                        last = MM(ps[:, SC + b // HALF, e - b - P:e - b], mcol[0:1, :], mrow[0:1, :], start=False, stop=True)
                last.then_inc(s_done, 1)

            def turn(h, qb):
                a = h * NB + qb
                pe.wait_ge(comb_done, a + 1)
                for b in range(qb + 1):
                    last = TR(ps[:, SC + b // HT, (b % HT) * P:(b % HT + 1) * P], prob[:, 0, b * P:(b + 1) * P], ident[:, :])
                last.then_inc(t_done, 1)

            def weighted(h, qb):
                a = h * NB + qb
                pe.wait_ge(at_done, a + 1)
                pe.wait_ge(v_ld, (a + 1) * 16)
                pe.wait_ge(ozf_ok, a)
                for b in range(qb + 1):
                    last = three(ps[:, OB, 0:VD], aT_hi[:, b], aT_lo[:, b], v_sb[:, b, 0], v_sb[:, b, 1], b == 0, b == qb)
                last.then_inc(pv_done, 1)

            def o_turn(h, qb):
                a = h * NB + qb
                pe.wait_ge(o_ok, a + 1)
                for m in range(2):
                    last = TR(ps[:, OB, VD + m * P:VD + (m + 1) * P], o_sb[:, m * P:(m + 1) * P], ident[:, :])
                last.then_inc(oT_done, 1)

            def step(h, cc, prev):
                ph, pc = (h, cc - 1) if cc else (h - 1, COLS - 1)
                G = h * COLS + cc
                scores(h - 1, cc, 0)
                pe.wait_ge(ev_done, (G - 1) * 2)
                unit(h, cc, 0)
                scores(h - 1, cc, 1)
                if prev:
                    o_turn(*((h - 1, cc - 1) if cc else (h - 2, NB - 1)))
                if pc // 2 == 2:
                    v_turn(ph, pc, 0)
                unit(h, cc, 1)
                if pc // 2 == 2:
                    v_turn(ph, pc, 1)
                unit(h, cc, 2)
                turn(h - 1, cc)
                unit(h, cc, 3)
                weighted(h - 1, cc)

            g = 0
            for cc in range(FIRST, COLS):
                pe.wait_ge(ev_done, 2 if cc == FIRST else 2 * (cc - 1))
                for j in range(UNITS):
                    unit(0, cc, j)
                    if (cc - 1) // 2 == 2 and j in (0, 1):
                        v_turn(0, cc - 1, j)
                    g += 1
                    if g % SUBS == 0 and g <= GCH * SUBS:
                        mod_sum(MCH + g // SUBS - 1)
                    if g == GCH * SUBS + 2:
                        pe.wait_ge(gp_ok, 1)
                        TR(ps[0:KT, OB, 0:P], mod[:, 2 * KT:3 * KT], ident[:, :]).then_inc(gp_mm, 1)
            pe.wait_ge(gp_cp, 1)
            for cc in range(COLS):
                step(1, cc, cc > 0)
            with pe.Fori(2, HEADS) as h:
                for cc in range(COLS):
                    step(h, cc, True)
            LH = HEADS - 1

            def tick(u):
                if u >= OUTS:
                    return
                G, k = divmod(u, KT)
                half = G // GROUPS
                if G % GROUPS == 0 and k % UK == 0:
                    pe.wait_ge(oz_ld[half * UNITS + k // UK], 2 * 16)
                if G % GROUPS == 0 and k == KT - 2:
                    pe.wait_ge(oz7_ok, (half + 1) * HT)
                if u == 0:
                    pe.wait_ge(ev_done, HEADS * COLS * 2)
                pe.wait_ge(w_split, U0 + u + 1)
                b_hi = w_hi[:, u % 2].rearrange("p a c -> p (a c)")
                b_lo = w_lo[:, u % 2].rearrange("p a c -> p (a c)")
                for t in range(HT):
                    if k == 0 and G:
                        pe.wait_ge(y_ok, (G - 1) * HT + t + 1)
                    tok = slice((half * HT + t) * P, (half * HT + t + 1) * P)
                    last = three(ps[:, t], hT_hi[:, k, tok], hT_lo[:, k, tok], b_hi, b_lo, k == 0, k == KT - 1)
                    if k == KT - 1 and t < HT - 1:
                        last.then_inc(out_done, 1)
                last.then_inc(w_used, 1)

            u = 0
            for qb in range(NB):
                n0, n1, n2 = SLOTS[qb]
                scores(LH, qb, 0)
                for i in range(n0):
                    tick(u + i)
                scores(LH, qb, 1)
                o_turn(*((LH, qb - 1) if qb else (LH - 1, NB - 1)))
                for i in range(n1):
                    tick(u + n0 + i)
                turn(LH, qb)
                for i in range(n2):
                    tick(u + n0 + n1 + i)
                weighted(LH, qb)
                u += n0 + n1 + n2
            tick(u)
            tick(u + 1)
            o_turn(LH, NB - 1)
            for v in range(u + 2, OUTS):
                tick(v)


_INS = ["x", "c", "ada_w", "ada_b", "norm_pre", "norm_post", "diff_w_in", "diff_w_out", "diff_lambda_q1",
        "diff_lambda_k1", "diff_lambda_q2", "diff_lambda_k2", "diff_subln"]


def kernel(**inputs):
    import numpy as _np
    import concourse.bacc as _bacc
    from concourse import mybir as _mybir
    from concourse.bass_utils import run_bass_kernel_spmd as _run

    nc = _bacc.Bacc("TRN2", target_bir_lowering=False, num_devices=1, dynamic_dma_scratch_size=1024)
    arrays, args = {}, []
    for name in _INS:
        a = _np.ascontiguousarray(inputs[name])
        arrays[f"in_{name}_dram"] = a
        args.append(nc.dram_tensor(f"in_{name}_dram", a.shape, _mybir.dt.from_np(a.dtype), kind="ExternalInput").ap())
    out = nc.dram_tensor("out_0_dram", inputs["x"].shape, _mybir.dt.float32, kind="ExternalOutput").ap()
    build(nc, *args, out)
    r = _run(nc, [arrays], core_ids=[0])
    return r.results[0]["out_0_dram"]
```
